# Optimizing a Trainium2 kernel written in Bass

```python
import math
import jax, jax.numpy as jnp
from jax import lax
import numpy as np

D_MODEL = 1024
BATCH = 1
SEQ = 256
DEPTH = 2

GRID_W = 64
N_BRANCH = 4
BRANCH_W = 512
EPS = 1e-6

DN_HEADS = 4
DN_DK = 128
DN_DV = 128
DN_CONV = 5
DN_CHUNK = 64
NA_HEADS = 8
NA_DH = 64
NA_ROWS = 8
NA_COLS = 16
GA_HEADS = 4
GA_KV_HEADS = 2
GA_DH = 128
GA_BLOCK = 128
ROPE_THETA = 10000.0
ML_HEADS = 4
ML_DK = 64
ML_DV = 128
ML_CHUNK = 64

PROJ_SIZES = (
    DN_HEADS * (2 * DN_DK + DN_DV),
    2 * DN_HEADS,
    2 * DN_HEADS,
    BRANCH_W,
    3 * NA_HEADS * NA_DH,
    BRANCH_W,
    GA_HEADS * GA_DH,
    GA_KV_HEADS * GA_DH,
    GA_KV_HEADS * GA_DH,
    BRANCH_W,
    ML_HEADS * ML_DK,
    ML_HEADS * ML_DK,
    ML_HEADS * ML_DV,
    2 * ML_HEADS,
    2 * ML_HEADS,
    ML_HEADS * ML_DV,
    BRANCH_W,
    N_BRANCH * D_MODEL,
)

kernel_name = "hybrid_gated_parallel_encoder"

F32 = jnp.float32

def _rms(x, g):
    xf = x.astype(F32)
    y = xf * lax.rsqrt(jnp.mean(xf * xf, axis=-1, keepdims=True) + EPS)
    return (y * g.astype(F32)).astype(x.dtype)

def _l2n(x):
    return x * lax.rsqrt(jnp.sum(x * x, axis=-1, keepdims=True) + EPS)

def _heads(x, h):
    B, S, _ = x.shape
    return x.reshape(B, S, h, -1).transpose(0, 2, 1, 3)

def _merge_heads(x):
    B, H, S, d = x.shape
    return x.transpose(0, 2, 1, 3).reshape(B, S, H * d)

def _split(p, sizes):
    out, o = [], 0
    for s in sizes:
        out.append(p[..., o:o + s])
        o += s
    return out

def _centred_conv(x, w):
    K = w.shape[0]
    S = x.shape[1]
    pad = K // 2
    xp = jnp.pad(x, ((0, 0), (pad, pad), (0, 0)))
    out = xp[:, 0:S] * w[0]
    for j in range(1, K):
        out = out + xp[:, j:j + S] * w[j]
    return out

def _gated_delta(q, k, v, g, beta):
    B, H, S, dk = q.shape
    dv = v.shape[-1]
    C = DN_CHUNK
    N = S // C
    q = q.reshape(B, H, N, C, dk)
    k = k.reshape(B, H, N, C, dk)
    v = v.reshape(B, H, N, C, dv)
    g = g.reshape(B, H, N, C)
    beta = beta.reshape(B, H, N, C)
    gc = jnp.cumsum(g, axis=-1)
    causal = jnp.tril(jnp.ones((C, C), bool))
    strict = jnp.tril(jnp.ones((C, C), bool), -1)
    diff = gc[..., :, None] - gc[..., None, :]
    decay = jnp.where(causal, jnp.exp(jnp.where(causal, diff, 0.0)), 0.0)
    kk = jnp.einsum('bhnid,bhnjd->bhnij', k, k)
    a_mat = jnp.eye(C, dtype=q.dtype) + jnp.where(strict, beta[..., :, None] * kk * decay, 0.0)
    rhs = jnp.concatenate([v * beta[..., None], k * (beta * jnp.exp(gc))[..., None]], axis=-1)
    sol = lax.linalg.triangular_solve(a_mat, rhs, left_side=True, lower=True, unit_diagonal=True)
    u, w = sol[..., :dv], sol[..., dv:]
    qk = jnp.einsum('bhnid,bhnjd->bhnij', q, k) * decay
    q_dec = q * jnp.exp(gc)[..., None]
    k_dec = k * jnp.exp(gc[..., -1:] - gc)[..., None]
    g_tot = jnp.exp(gc[..., -1])
    xs = tuple(jnp.moveaxis(t, 2, 0) for t in (qk, q_dec, k_dec, u, w, g_tot))

    def step(state, inp):
        qk_n, qd_n, kd_n, u_n, w_n, gt_n = inp
        v_new = u_n - jnp.einsum('bhcd,bhde->bhce', w_n, state)
        o = jnp.einsum('bhcd,bhde->bhce', qd_n, state) + jnp.einsum('bhij,bhje->bhie', qk_n, v_new)
        state = state * gt_n[..., None, None] + jnp.einsum('bhcd,bhce->bhde', kd_n, v_new)
        return state, o

    s0 = jnp.zeros((B, H, dk, dv), q.dtype)
    _, o = lax.scan(step, s0, xs)
    return jnp.moveaxis(o, 0, 2).reshape(B, H, S, dv)

def _mixer_deltanet(qkv, a_pre, b_pre, z, conv_w, a_log, dt_bias, norm_g):
    B, S, _ = qkv.shape
    qkv = jax.nn.silu(_centred_conv(qkv, conv_w))
    q, k, v = _split(qkv, (DN_HEADS * DN_DK, DN_HEADS * DN_DK, DN_HEADS * DN_DV))
    q = _l2n(_heads(q, DN_HEADS).astype(F32)) * (DN_DK ** -0.5)
    k = _l2n(_heads(k, DN_HEADS).astype(F32))
    v = _heads(v, DN_HEADS).astype(F32)
    a_pre = a_pre.reshape(B, S, 2, DN_HEADS).transpose(2, 0, 3, 1).astype(F32)
    b_pre = b_pre.reshape(B, S, 2, DN_HEADS).transpose(2, 0, 3, 1).astype(F32)
    g = -jnp.exp(a_log.astype(F32))[:, None, :, None] * jax.nn.softplus(a_pre + dt_bias.astype(F32)[:, None, :, None])
    beta = jax.nn.sigmoid(b_pre)
    o_f = _gated_delta(q, k, v, g[0], beta[0])
    fl = lambda t: jnp.flip(t, axis=2)
    o_b = fl(_gated_delta(fl(q), fl(k), fl(v), fl(g[1]), fl(beta[1])))
    o = _rms(o_f + o_b, norm_g)
    return _merge_heads(o).astype(z.dtype) * jax.nn.silu(z)

def _neighbourhood_attention(q, k, v, rpb):
    B, H, S, dh = q.shape
    rows = S // GRID_W
    kr = min(NA_ROWS, rows)
    qg = q.reshape(B, H, rows, GRID_W, dh)
    kg = k.reshape(B, H, rows, GRID_W, dh)
    vg = v.reshape(B, H, rows, GRID_W, dh)
    r = jnp.arange(rows)
    r0 = jnp.clip(r - kr // 2, 0, rows - kr)
    key_rows = r0[:, None] + jnp.arange(kr)[None, :]
    kw = kg[:, :, key_rows]
    vw = vg[:, :, key_rows]
    s = jnp.einsum('bhrqd,bhrkwd->bhrqkw', qg, kw).astype(F32) * (dh ** -0.5)
    c = jnp.arange(GRID_W)
    c0 = jnp.clip(c - NA_COLS // 2, 0, GRID_W - NA_COLS)
    in_win = (c[None, :] >= c0[:, None]) & (c[None, :] < c0[:, None] + NA_COLS)
    row_off = key_rows - r[:, None] + NA_ROWS - 1
    col_off = jnp.clip(c[None, :] - c[:, None], -(NA_COLS - 1), NA_COLS - 1) + NA_COLS - 1
    bias = rpb[:, row_off[:, None, :, None], col_off[None, :, None, :]]
    s = jnp.where(in_win[:, None, :], s + bias[None].astype(F32), -jnp.inf)
    p = jax.nn.softmax(s.reshape(B, H, rows, GRID_W, kr * GRID_W), axis=-1)
    p = p.reshape(B, H, rows, GRID_W, kr, GRID_W).astype(v.dtype)
    o = jnp.einsum('bhrqkw,bhrkwd->bhrqd', p, vw)
    return o.reshape(B, H, S, dh)

def _mixer_natten(qkv, z, q_g, k_g, rpb):
    q, k, v = _split(qkv, (NA_HEADS * NA_DH,) * 3)
    q = _rms(_heads(q, NA_HEADS), q_g)
    k = _rms(_heads(k, NA_HEADS), k_g)
    v = _heads(v, NA_HEADS)
    o = _neighbourhood_attention(q, k, v, rpb)
    return _merge_heads(o) * jax.nn.silu(z)

def _rope_tables(S, dtype):
    t = jnp.arange(S)
    row = (t // GRID_W).astype(F32)
    col = (t % GRID_W).astype(F32)
    m = GA_DH // 4
    inv = ROPE_THETA ** (-jnp.arange(m, dtype=F32) / m)
    ar = row[:, None] * inv
    ac = col[:, None] * inv
    return (jnp.cos(ar).astype(dtype), jnp.sin(ar).astype(dtype),
            jnp.cos(ac).astype(dtype), jnp.sin(ac).astype(dtype))

def _rope_axis(x, cos, sin):
    m = x.shape[-1] // 2
    x1, x2 = x[..., :m], x[..., m:]
    return jnp.concatenate([x1 * cos - x2 * sin, x1 * sin + x2 * cos], axis=-1)

def _axial_rope(x, cr, sr, cc, sc):
    half = x.shape[-1] // 2
    return jnp.concatenate([_rope_axis(x[..., :half], cr, sr), _rope_axis(x[..., half:], cc, sc)], axis=-1)

def _gqa_blocked(q, k, v):
    B, Hk, G, S, dh = q.shape
    nb = S // GA_BLOCK
    qb = q.reshape(B, Hk, G, nb, GA_BLOCK, dh).transpose(3, 0, 1, 2, 4, 5)

    def one(qi):
        s = jnp.einsum('bkgqd,bksd->bkgqs', qi, k).astype(F32) * (dh ** -0.5)
        p = jax.nn.softmax(s, axis=-1).astype(v.dtype)
        return jnp.einsum('bkgqs,bksd->bkgqd', p, v)

    o = lax.map(one, qb)
    return o.transpose(1, 2, 3, 0, 4, 5).reshape(B, Hk * G, S, dh)

def _mixer_gqa(q, k, v, z, q_g, k_g, rope):
    B, S, _ = q.shape
    q = _axial_rope(_rms(_heads(q, GA_HEADS), q_g), *rope)
    k = _axial_rope(_rms(_heads(k, GA_KV_HEADS), k_g), *rope)
    v = _heads(v, GA_KV_HEADS)
    q = q.reshape(B, GA_KV_HEADS, GA_HEADS // GA_KV_HEADS, S, GA_DH)
    o = _gqa_blocked(q, k, v)
    return _merge_heads(o) * jax.nn.silu(z)

def _mlstm_chunked(q, k, v, ig, lf):
    B, H, S, dk = q.shape
    dv = v.shape[-1]
    C = ML_CHUNK
    N = S // C
    q = q.reshape(B, H, N, C, dk)
    k = k.reshape(B, H, N, C, dk)
    v = v.reshape(B, H, N, C, dv)
    ig = ig.reshape(B, H, N, C)
    bcum = jnp.cumsum(lf.reshape(B, H, N, C), axis=-1)
    xs = tuple(jnp.moveaxis(t, 2, 0) for t in (q, k, v, ig, bcum))
    causal = jnp.tril(jnp.ones((C, C), bool))

    def step(carry, inp):
        c_st, n_st, m_st = carry
        q_n, k_n, v_n, ig_n, b_n = inp
        d_log = jnp.where(causal, b_n[..., :, None] - b_n[..., None, :] + ig_n[..., None, :], -jnp.inf)
        m_inter = b_n + m_st[..., None]
        m = jnp.maximum(jnp.max(d_log, axis=-1), m_inter)
        s = jnp.einsum('bhid,bhjd->bhij', q_n, k_n) * jnp.exp(d_log - m[..., None])
        inter = jnp.exp(m_inter - m)
        numer = inter[..., None] * jnp.einsum('bhid,bhde->bhie', q_n, c_st) + jnp.einsum('bhij,bhje->bhie', s, v_n)
        denom = inter * jnp.einsum('bhid,bhd->bhi', q_n, n_st) + jnp.sum(s, axis=-1)
        h = numer / jnp.maximum(jnp.abs(denom), jnp.exp(-m))[..., None]
        b_last = b_n[..., -1]
        w_log = b_last[..., None] - b_n + ig_n
        m_new = jnp.maximum(b_last + m_st, jnp.max(w_log, axis=-1))
        dec = jnp.exp(b_last + m_st - m_new)
        wk = k_n * jnp.exp(w_log - m_new[..., None])[..., None]
        c_st = dec[..., None, None] * c_st + jnp.einsum('bhcd,bhce->bhde', wk, v_n)
        n_st = dec[..., None] * n_st + jnp.sum(wk, axis=-2)
        return (c_st, n_st, m_new), h

    init = (jnp.zeros((B, H, dk, dv), q.dtype), jnp.zeros((B, H, dk), q.dtype), jnp.zeros((B, H), q.dtype))
    _, h = lax.scan(step, init, xs)
    return jnp.moveaxis(h, 0, 2).reshape(B, H, S, dv)

def _mixer_mlstm(q, k, v, i_pre, f_pre, o_pre, z, i_bias, f_bias, norm_g):
    B, S, _ = q.shape
    q = _heads(q, ML_HEADS).astype(F32)
    k = _heads(k, ML_HEADS).astype(F32) * (ML_DK ** -0.5)
    v = _heads(v, ML_HEADS).astype(F32)
    ig = i_pre.reshape(B, S, 2, ML_HEADS).transpose(2, 0, 3, 1).astype(F32) + i_bias.astype(F32)[:, None, :, None]
    lf = jax.nn.log_sigmoid(f_pre.reshape(B, S, 2, ML_HEADS).transpose(2, 0, 3, 1).astype(F32)
                            + f_bias.astype(F32)[:, None, :, None])
    h_f = _mlstm_chunked(q, k, v, ig[0], lf[0])
    fl = lambda t: jnp.flip(t, axis=2)
    h_b = fl(_mlstm_chunked(fl(q), fl(k), fl(v), fl(ig[1]), fl(lf[1])))
    h = _merge_heads(_rms(h_f + h_b, norm_g)).astype(z.dtype)
    return jax.nn.sigmoid(o_pre) * h * jax.nn.silu(z)

def setup_inputs(seed: int = 0) -> dict:
    key = jax.random.key(seed)
    ks = jax.random.split(key, 18)

    def nrm(k, shape, s):
        return s * jax.random.normal(k, shape, F32)

    proj_w = sum(PROJ_SIZES)
    dt = jnp.exp(jax.random.uniform(ks[5], (DEPTH, 2, DN_HEADS), F32, math.log(1e-3), math.log(1e-1)))
    return {
        "x": jax.random.normal(ks[0], (BATCH, SEQ, D_MODEL), F32),
        "norm_g": 1.0 + nrm(ks[1], (DEPTH, D_MODEL), 0.02),
        "w_in": nrm(ks[2], (DEPTH, D_MODEL, proj_w), D_MODEL ** -0.5),
        "conv_a": nrm(ks[3], (DEPTH, DN_CONV, DN_HEADS * (2 * DN_DK + DN_DV)), DN_CONV ** -0.5),
        "dn_a_log": jnp.log(jax.random.uniform(ks[4], (DEPTH, 2, DN_HEADS), F32, 1.0, 16.0)),
        "dn_dt_bias": dt + jnp.log(-jnp.expm1(-dt)),
        "dn_norm_g": 1.0 + nrm(ks[6], (DEPTH, DN_DV), 0.02),
        "na_q_norm": 1.0 + nrm(ks[7], (DEPTH, NA_DH), 0.02),
        "na_k_norm": 1.0 + nrm(ks[8], (DEPTH, NA_DH), 0.02),
        "na_rpb": nrm(ks[9], (DEPTH, NA_HEADS, 2 * NA_ROWS - 1, 2 * NA_COLS - 1), 0.02),
        "ga_q_norm": 1.0 + nrm(ks[10], (DEPTH, GA_DH), 0.02),
        "ga_k_norm": 1.0 + nrm(ks[11], (DEPTH, GA_DH), 0.02),
        "ml_i_bias": nrm(ks[12], (DEPTH, 2, ML_HEADS), 0.1),
        "ml_f_bias": jax.random.uniform(ks[13], (DEPTH, 2, ML_HEADS), F32, 3.0, 6.0),
        "ml_norm_g": 1.0 + nrm(ks[14], (DEPTH, ML_DV), 0.02),
        "w_branch": nrm(ks[15], (DEPTH, N_BRANCH, BRANCH_W, D_MODEL), BRANCH_W ** -0.5),
        "w_out": nrm(ks[16], (DEPTH, D_MODEL, D_MODEL), D_MODEL ** -0.5),
    }

def reference(x, norm_g, w_in, conv_a, dn_a_log, dn_dt_bias, dn_norm_g, na_q_norm, na_k_norm, na_rpb,
              ga_q_norm, ga_k_norm, ml_i_bias, ml_f_bias, ml_norm_g, w_branch, w_out):
    B, S, _ = x.shape
    rope = _rope_tables(S, x.dtype)
    for l in range(DEPTH):
        h = _rms(x, norm_g[l])
        p = jnp.einsum('bsd,de->bse', h, w_in[l])
        (a_qkv, a_a, a_b, a_z, b_qkv, b_z, c_q, c_k, c_v, c_z,
         d_q, d_k, d_v, d_i, d_f, d_o, d_z, gate_logits) = _split(p, PROJ_SIZES)
        y_a = _mixer_deltanet(a_qkv, a_a, a_b, a_z, conv_a[l], dn_a_log[l], dn_dt_bias[l], dn_norm_g[l])
        y_b = _mixer_natten(b_qkv, b_z, na_q_norm[l], na_k_norm[l], na_rpb[l])
        y_c = _mixer_gqa(c_q, c_k, c_v, c_z, ga_q_norm[l], ga_k_norm[l], rope)
        y_d = _mixer_mlstm(d_q, d_k, d_v, d_i, d_f, d_o, d_z, ml_i_bias[l], ml_f_bias[l], ml_norm_g[l])
        ys = jnp.stack([y_a, y_b, y_c, y_d], axis=2)
        proj = jnp.einsum('bsnw,nwd->bsnd', ys, w_branch[l])
        gates = jax.nn.sigmoid(gate_logits.reshape(B, S, N_BRANCH, D_MODEL))
        merged = jnp.sum(gates * proj, axis=2)
        x = x + jnp.einsum('bsd,de->bse', merged, w_out[l])
    return x


_drawn_inputs = setup_inputs


def setup_inputs(seed=0):
    import zlib

    import numpy as np

    out = dict(_drawn_inputs(seed))
    spreads = {}
    factors = {'dn_norm_g': 5.96,
     'na_q_norm': 8.0,
     'na_k_norm': 8.0,
     'na_rpb': 64.0,
     'ga_q_norm': 8.0,
     'ga_k_norm': 8.0,
     'ml_i_bias': 8.0,
     'ml_norm_g': 8.0}
    for name, (base, spread) in spreads.items():
        noise = np.random.default_rng([zlib.crc32(name.encode()), seed]).standard_normal(out[name].shape)
        drawn = base * np.exp(spread * noise) if base else spread * noise
        out[name] = __import__('jax').numpy.asarray(drawn.astype(out[name].dtype))
    for name, factor in factors.items():
        out[name] = (out[name] * factor).astype(out[name].dtype)
    return out
```

```python
from contextlib import ExitStack

import numpy as np

import concourse.bass as bass
from concourse import mybir

F32 = mybir.dt.float32
ALU = mybir.AluOpType
ACT = mybir.ActivationFunctionType
X = mybir.AxisListType.X

P = 128
D = 1024
S = 256
DEPTH = 2
NT = S // P
KT = D // P
BW = 512
BK = BW // P
EPS = 1e-6
H = 4
HD = 128
C = 64
STEPS = S // C
NAH, NAD = 8, 64
WIN, GRID = 16, 64
RPB_R, RPB_C = 15, 31
MLK = 64
CONV = 5
CB = 12
LEVELS = 6
BIG = 1e30

A_QKV, A_AB, A_Z = 0, 1536, 1552
B_QKV, B_Z = 2064, 3600
C_QKV, C_Z = 4112, 5136
D_QKV, D_IF, D_O, D_Z = 5648, 6672, 6688, 7200
GATES = 7712
PW = 11808
WB = 256
SLOTS = 3

TILE_OF = (0, 1, 1, 0)
KIND_OF = (0, 0, 1, 1)
CHUNKS = ((0, 3), (1, 2))
BRANCHES = (0, 2, 1, 3)


def half_of(direction, s):
    return direction ^ KIND_OF[s]


def constants():
    i = np.arange(P)
    same = (i[:, None] // C) == (i[None, :] // C)
    lo = (i[:, None] < C) & same
    hi = (i[:, None] >= C) & same
    le, ge = i[:, None] <= i[None, :], i[:, None] >= i[None, :]
    before = [(lo & le) | (hi & ge), (lo & ge) | (hi & le)]
    eye = np.eye(P, dtype=bool)
    out = {"ident": eye, "ones": np.ones((P, P))}
    for k in range(2):
        out[f"cum{k}"] = before[k]
        out[f"after{k}"] = before[1 - k] & ~eye
        out[f"mask{k}"] = np.where(before[1 - k], 0.0, -BIG)
    out["half0"] = np.repeat(i[:, None] < C, P, axis=1)
    out["half1"] = np.repeat(i[:, None] >= C, P, axis=1)
    for k in range(2):
        for n in range(LEVELS):
            b = (i % C) >> n
            down = (b[:, None] % 2 == 1) & (b[None, :] == b[:, None] - 1)
            out[f"level{k}_{n}"] = (lo & down) | (hi & down.T) if k == 0 else (lo & down.T) | (hi & down)
    tokens = np.stack([np.concatenate([np.arange(C) + C * c for c in CHUNKS[t]]) for t in range(NT)])
    m = HD // 4
    inv = (np.float32(10000.0) ** (-np.arange(m, dtype=np.float32) / np.float32(m))).astype(np.float32)
    row = (tokens // GRID).astype(np.float32)[..., None] * inv
    col = (tokens % GRID).astype(np.float32)[..., None] * inv
    cos = np.concatenate([np.cos(row), np.cos(row), np.cos(col), np.cos(col)], -1)
    sin = np.concatenate([-np.sin(row), np.sin(row), -np.sin(col), np.sin(col)], -1)
    out["cos"] = cos.transpose(1, 0, 2).reshape(P, NT * HD)
    out["sin"] = sin.transpose(1, 0, 2).reshape(P, NT * HD)
    c = np.arange(GRID)
    c0 = np.clip(c - WIN // 2, 0, GRID - WIN)
    win = (c[None, :] >= c0[:, None]) & (c[None, :] < c0[:, None] + WIN)
    out["window"] = np.tile(np.where(win, 0.0, -BIG), (2, 1))
    z = (np.arange(P)[:, None] + np.arange(P)[None, :] == 78) & (np.arange(P)[:, None] < RPB_C)
    out["toeplitz"] = z
    pick = np.zeros((P, NAH * 7))
    for h in range(NAH):
        for o in range(7):
            pick[h * RPB_R + 4 + o, h * 7 + o] = 1
    out["pick"] = pick
    return {k: np.asarray(v, np.float32) for k, v in out.items()}


def const_layout():
    at, where = 0, {}
    for name, a in constants().items():
        where[name] = (at, a.shape[1])
        at += a.shape[1]
    return where, at


def weight_plan():
    plan = [("conv", i, A_QKV + WB * i) for i in range(6)]
    plan += [("za", i, A_Z + WB * i) for i in range(2)]
    plan += [("c", i, C_QKV + WB * i) for i in range(4)]
    plan += [("zc", i, C_Z + WB * i) for i in range(2)]
    plan += [("b", i, B_QKV + WB * i) for i in range(6)]
    plan += [("zb", i, B_Z + WB * i) for i in range(2)]
    plan += [("d", i, D_QKV + WB * i) for i in range(4)]
    plan += [("o", i, D_O + WB * i) for i in range(2)]
    plan += [("zd", i, D_Z + WB * i) for i in range(2)]
    for n in BRANCHES:
        for c in range(2):
            plan += [("gate", (n, c, i), GATES + n * D + c * 512 + WB * i) for i in range(2)]
            plan += [("branch", (n, c), c * 512)]
    plan += [("out", i, WB * i) for i in range(4)]
    return plan


def order():
    def weave(main, fill):
        n, out = max(len(main), len(fill)), []
        for i in range(n):
            out += main[i * len(main) // n:(i + 1) * len(main) // n]
            out += fill[i * len(fill) // n:(i + 1) * len(fill) // n]
        return out

    def gate(n, c):
        return [("proj", "gate", (n, c, 0)), ("proj", "gate", (n, c, 1)), ("branch", n, c)]

    o = [("norm",), ("gatecols",)]
    o += [("proj", "conv", 0)]
    for i in range(1, 6):
        o += [("proj", "conv", i), ("conv", i - 1)]
    o += [("cols",), ("conv", 5), ("proj", "za", 0), ("a_turn",), ("proj", "za", 1), ("a_norm",), ("proj", "c", 0),
          ("a_qkt",)]
    a = [("rows", s) for s in range(STEPS)]
    for s in (0, 2):
        a += [("solve0", s), ("solve0", s + 1)]
        for n in range(1, LEVELS):
            a += [("t1", s, n), ("t1", s + 1, n), ("update", s, n), ("update", s + 1, n)]
        a += [("uw", s), ("uw", s + 1), ("scan_v", s), ("scan_o", s), ("scan_v", s + 1), ("scan_o", s + 1)]
    a += [("a_sum", 0), ("a_sum", 1), ("a_out", 0), ("a_out", 1)]
    fill = [("proj", "c", i) for i in range(1, 4)] + [("proj", "zc", i) for i in range(2)] + [("c_prep",), ("proj", "b", 0)]
    for i, (t, g) in enumerate(((0, 0), (0, 1), (1, 0), (1, 1))):
        fill += [("c_score", t, g), ("proj", "b", i + 1), ("c_turn", t, g), ("c_mix", t, g)]
    fill += [("c_sum", 0), ("c_sum", 1), ("proj", "b", 5), ("c_out", 0), ("c_out", 1)]
    fill += [("proj", k, i) for k, n in (("zb", 2), ("d", 4), ("o", 2), ("zd", 2)) for i in range(n)]
    o += weave(a, fill)
    b = [("b_bias", i) for i in range(8)] + [("b_prep",)]
    for t in range(NT):
        for g in range(2):
            b += [("b_score", t, g), ("b_turn", t, g)]
    b += [("b_sum", 0), ("b_sum", 1), ("b_out", 0), ("b_out", 1)]
    d = [("d_prep",)] + [("d_rows", s) for s in range(STEPS)] + [("d_m",)] + [("d_step", s) for s in range(STEPS)]
    d += [("d_scan", s) for s in range(STEPS)] + [("d_den",), ("d_sum", 0), ("d_sum", 1), ("d_out", 0), ("d_out", 1)]
    o += weave(b + d, [g for n in BRANCHES[:2] for c in range(2) for g in gate(n, c)])
    o += [g for n in BRANCHES[2:] for c in range(2) for g in gate(n, c)]
    o += [("merged",)] + [("proj", "out", i) for i in range(4)]
    return o


def build(nc, x_in, norm_g, w_in, conv_a, dn_a_log, dn_dt_bias, dn_norm_g, na_q_norm, na_k_norm, na_rpb,
          ga_q_norm, ga_k_norm, ml_i_bias, ml_f_bias, ml_norm_g, w_branch, w_out, table, out):
    ctx = ExitStack()
    with ctx:
        def sb(name, *free):
            return ctx.enter_context(nc.sbuf_tensor(name, [P, *free], F32))

        class Region:

            def __init__(self, t, at, size):
                self.t, self.at, self.size = t, at, size

            def cut(self, **dims):
                n = int(np.prod(list(dims.values())))
                assert self.at + n <= self.size, (self.at + n, self.size)
                v = self.t[:, self.at:self.at + n]
                self.at += n
                names = " ".join(dims)
                return v if len(dims) == 1 else v.rearrange(f"p ({names}) -> p {names}", **dims)

        where, n_const = const_layout()
        tab = sb("tab", n_const)

        def K(name):
            a, n = where[name]
            return tab[:, a:a + n]

        def over(v, n):
            return v[:, None, :].to_broadcast([v.shape[0], n, v.shape[1]])

        def along(v, n):
            return v[:, :, None].to_broadcast([v.shape[0], v.shape[1], n])

        x = sb("x", NT, D)
        hT = sb("hT", KT, S)
        ring = sb("ring", SLOTS, KT * WB)
        zbuf = sb("zbuf", 4, NT, BW)
        z = [zbuf[:, k] for k in (0, 2, 1, 3)]
        merged = zbuf[:, 0:2]
        yT = [sb("yT0", BK, S)[:], None, sb("yT2", BK, S)[:], None]
        n_small = 2000
        small = Region(sb("small", n_small), 0, n_small)
        colp = small.cut(a=CONV * CB + KT)
        g_dn, g_ml = small.cut(a=HD), small.cut(a=HD)
        g_nq, g_nk = small.cut(a=NAD), small.cut(a=NAD)
        g_gate = small.cut(k=4, e=8)
        neg_half = small.cut(a=32)
        ssx, rsx = small.cut(a=NT), small.cut(a=NT)
        gps = small.cut(t=NT, e=32)
        raw = small.cut(t=NT, k=4, e=8)
        softp = small.cut(t=NT, k=2, e=8)
        coef = small.cut(k=2, e=8)
        sel = small.cut(s=STEPS, k=4, h=H)
        cc = small.cut(w=4, s=STEPS, e=8)
        ex = small.cut(w=4, s=STEPS, e=8)
        av = small.cut(s=STEPS, h=H)
        bev = small.cut(s=STEPS, h=H)
        hbeta = small.cut(s=STEPS, h=H)
        amx = small.cut(s=STEPS, h=H, k=2)
        cm = small.cut(s=STEPS, h=H)
        mst = small.cut(s=STEPS, k=2, h=H)
        mxs = small.cut(s=STEPS, k=2, h=H)
        msel, mxsel = small.cut(s=STEPS, h=H), small.cut(s=STEPS, h=H)
        mrun = small.cut(s=STEPS, h=H)
        e_in, e_out = small.cut(k=3, s=STEPS, h=H), small.cut(k=3, s=STEPS, h=H)
        dec_in, dec = small.cut(s=STEPS, k=2, h=H), small.cut(s=STEPS, k=2, h=H)
        decp = small.cut(s=STEPS, k=2, u=2)
        ssa, rsa = small.cut(t=NT, g=8), small.cut(t=NT, g=8)
        ssb, rsb = small.cut(t=NT, g=16), small.cut(t=NT, g=16)
        ssc, rsc = small.cut(t=NT, g=6), small.cut(t=NT, g=6)
        nmc, smc, rmc = small.cut(t=NT, h=H), small.cut(t=NT, h=H), small.cut(t=NT, h=H)
        nmb, smb, rmb = small.cut(t=NT, h=NAH), small.cut(t=NT, h=NAH), small.cut(t=NT, h=NAH)
        sso, rso = small.cut(b=4, h=H), small.cut(b=4, h=H)
        rpbT = small.cut(a=NAH * 7)
        den, nden = small.cut(s=STEPS, h=H), small.cut(s=STEPS, h=H)

        n_big = 19504
        big = sb("big", n_big)
        r = Region(big, 0, n_big)
        cin = r.cut(b=CB, n=S + CONV - 1)
        cac = r.cut(b=CB, n=S)
        q = Region(big, 0, r.at)
        sX, sXT = q.cut(j=2, h=H, n=P), q.cut(j=2, h=H, n=P)
        sLT, sT1 = q.cut(j=2, h=H, n=P), q.cut(j=2, h=H, n=P)
        sLm = q.cut(j=2, h=H, n=P)
        vn = q.cut(h=H, n=P)
        vk = r.cut(w=2, h=H, n=P)
        tm = r.cut(t=NT, n=3 * BW)
        qkt = r.cut(g=8, n=S)
        us = qkt.rearrange("p (s g) n -> p s (g n)", s=STEPS).rearrange("p s (h n) -> p s h n", h=H)
        kkqk = r.cut(t=NT, w=2, h=H, n=P)
        qdT, kd = kkqk[:, 0], kkqk[:, 1]
        lw = r.cut(s=STEPS, h=H, n=P)
        qkd = r.cut(s=STEPS, h=H, n=P)
        csl = big[:, r.at - 4096:r.at - 1024].rearrange("p (b n) -> p b n", b=CB)
        st = r.cut(d=2, h=H, n=P)
        r = Region(big, 0, n_big)
        bias = r.cut(t=NT, h=NAH, n=S)
        nqT, nkT = r.cut(g=4, n=S), r.cut(g=4, n=S)
        yT[1], yT[3] = r.cut(g=BK, n=S), r.cut(g=BK, n=S)
        mqk_T = r.cut(t=NT, g=4, n=P)
        mqk = r.cut(t=NT, h=H, n=P)
        mS = r.cut(s=STEPS, h=H, n=P)
        mqT = r.cut(s=STEPS, g=2, n=P)
        mq = r.cut(s=STEPS, h=H, n=MLK)
        wk = r.cut(s=STEPS, h=H, n=MLK)
        cst = r.cut(d=2, g=2, n=HD + 1)
        num = r.cut(s=STEPS, h=H, n=HD + 1)
        n_mid = 8192
        mid = sb("mid", n_mid)
        r = Region(mid, 0, n_mid)
        ctm = r.cut(t=NT, n=1024)
        xh = ctm
        crp = r.cut(t=NT, n=768)
        cqT = r.cut(g=6, n=S)
        rope = r.cut(w=4, t=NT, n=HD)
        graw = r.cut(w=4, n=HD)
        prob = r.cut(j=2, g=2, n=S)
        probT = r.cut(g=2, k=2, n=P)
        r = Region(mid, r.at - 512, n_mid)
        w_ab, w_if = r.cut(k=KT, n=16), r.cut(k=KT, n=16)
        rawp = r.cut(a=P)
        rpb = r.cut(a=RPB_C)
        btm = sb("btm", NT, 3 * BW)
        r = Region(mid, 0, n_mid)
        dtm = r.cut(t=NT, n=512)
        vaug = r.cut(t=NT, h=H, n=HD + 1)
        gact0 = r.cut(t=NT, n=512)
        og = rope.rearrange("p w t n -> p (w t n)").rearrange("p (t n) -> p t n", t=NT)
        assert r.at <= 2048 + 1536
        gact = [gact0, cqT.rearrange("p g n -> p (g n)")[:, 0:1024].rearrange("p (t n) -> p t n", t=NT)]
        mtmp = graw.rearrange("p w n -> p (w n)")

        layer_sems = []

        def sem(name):
            s = ctx.enter_context(nc.semaphore(name))
            layer_sems.append(s)
            return s

        class Bank:

            def __init__(self, name):
                self.t = ctx.enter_context(nc.psum_tensor(name, [P, 512], F32))[:, :]
                self.full, self.free, self.fills = sem(name + "_full"), sem(name + "_free"), 0

        pj = [Bank("pj0"), Bank("pj1")]
        mb = [Bank(f"mb{i}") for i in range(6)]
        filling = {}

        def room(bank, key):
            assert key not in filling
            filling[key] = (bank, bank.fills + 1)
            bank.fills += 1
            return bank.free, bank.fills - 1

        def filled(key):
            bank, n = filling[key]
            return bank.full, n

        def released(key):
            bank, n = filling[key]
            return bank.free, n

        def bank_of(key):
            return filling[key][0]

        table_in = ctx.enter_context(nc.semaphore("table_in"))
        x_loaded = ctx.enter_context(nc.semaphore("x_loaded"))
        stored = ctx.enter_context(nc.semaphore("stored"))
        setup_done = ctx.enter_context(nc.semaphore("setup_done"))
        ring_full = [sem(f"ring_full{i}") for i in range(SLOTS)]
        weights_used = sem("weights_used")
        cols_in = sem("cols_in")
        params_in = sem("params_in")
        act_chain = sem("act_chain")
        dve_chain = sem("dve_chain")
        pool_chain = sem("pool_chain")
        x_squared = sem("x_squared")
        rms_x = sem("rms_x")
        h_ready = sem("h_ready")
        conv_out = sem("conv_out")
        conv_act = sem("conv_act")
        silu_ready = sem("silu_ready")
        z_tanh = sem("z_tanh")
        softplus_in = sem("softplus_in")
        gate_exp = sem("gate_exp")
        gates_ready = sem("gates_ready")
        selected = sem("selected")
        sums_ready = sem("sums_ready")
        terms_ready = sem("terms_ready")
        squared_a = sem("squared_a")
        summed_a = sem("summed_a")
        rms_a = sem("rms_a")
        normed_a = sem("normed_a")
        diag_ready = sem("diag_ready")
        decay_arg = sem("decay_arg")
        decay_ready = sem("decay_ready")
        decay_beta = sem("decay_beta")
        l_ready = sem("l_ready")
        x0_ready = sem("x0_ready")
        lm_ready = sem("lm_ready")
        scaled_uw = sem("scaled_uw")
        vn_ready = sem("vn_ready")
        st_decayed = sem("st_decayed")
        rope_ready = sem("rope_ready")
        squared_c = sem("squared_c")
        summed_c = sem("summed_c")
        rms_c = sem("rms_c")
        rotated = sem("rotated")
        c_max = sem("c_max")
        squared_b = sem("squared_b")
        summed_b = sem("summed_b")
        rms_b = sem("rms_b")
        scaled_b = sem("scaled_b")
        gained_b = sem("gained_b")
        b_max = sem("b_max")
        b_prob = sem("b_prob")
        y_in = sem("y_in")
        squared_y = sem("squared_y")
        summed_y = sem("summed_y")
        rms_y = sem("rms_y")
        scaled_y = sem("scaled_y")
        gained_y = sem("gained_y")
        y_ready = sem("y_ready")
        ones_ready = sem("ones_ready")
        diag2_ready = sem("diag2_ready")
        m_args = sem("m_args")
        m_exp = sem("m_exp")
        m_terms = sem("m_terms")
        s_arg = sem("s_arg")
        s_exp = sem("s_exp")
        s_ready = sem("s_ready")
        scaled_d = sem("scaled_d")
        c_decayed = sem("c_decayed")
        merged_first = sem("merged_first")
        merge_done = sem("merge_done")

        plan = weight_plan()
        block_no = {(k, a): n for n, (k, a, _) in enumerate(plan)}
        stages = order()
        ident, ones = K("ident"), K("ones")
        PARAM_DMAS = 15

        def rows_of(half):
            return slice(half * C, half * C + C)

        def heads(v, n):
            return v.rearrange("p (h n) -> p h n", h=n)

        def solve_no(s, n):
            return (s // 2) * 2 * (LEVELS - 1) + (n - 1) * 2 + s % 2

        def group_no(t, k):
            return t * 2 + k

        y_order = [a for a in stages if a[0] in ("a_out", "b_out", "c_out", "d_out")]
        y_no = {a: n for n, a in enumerate(y_order)}
        sum_order = [a for a in stages if a[0] in ("a_sum", "d_sum")]
        sum_no = {a: n for n, a in enumerate(sum_order)}
        z_order = [a[1:] for a in stages if a[0] == "proj" and a[1] in ("za", "zb", "zc", "zd")]
        z_no = {a: n for n, a in enumerate(z_order)}
        branch_list = [a[1:] for a in stages if a[0] == "branch"]
        branch_no = {(n, c): i for i, (n, c) in enumerate(a[1:] for a in stages if a[0] == "branch")}
        o_sum = {"a": [us[:, 0], us[:, 1]], "d": [mqk[:, 0], mqk[:, 1]]}
        o_sq = {"a": [us[:, 3], us[:, 2]], "d": [mqk_T[:, 0], mqk_T[:, 1]]}
        y_tile = {"a": [v.rearrange("p h n -> p (h n)") for v in o_sum["a"]],
                  "d": [v.rearrange("p h n -> p (h n)") for v in o_sum["d"]],
                  "b": [btm[:, t, 0:BW] for t in range(NT)], "c": [crp[:, t, 0:BW] for t in range(NT)]}
        probTs = [probT, mq.rearrange("p s h n -> p (s h n)")[:, 0:512].rearrange("p (g k n) -> p g k n", g=2, k=2)]
        pj_of = {}
        turn = 0
        for a in stages:
            if a[0] == "proj":
                pj_of[a] = turn % 2
                turn += 1
            elif a[0] == "branch":
                pj_of[a] = turn % 2

        def run(**steps):
            for name, *args in stages:
                if name in steps:
                    steps[name](*args)

        with nc.Block() as block:
            @block.sync
            def _(sp):
                sp.dma_start(tab[:, :], table).then_inc(table_in, 16)
                for t in range(NT):
                    for half in range(2):
                        c = CHUNKS[t][half]
                        sp.dma_start(x[rows_of(half), t, :], x_in[0, c * C:c * C + C, :]).then_inc(x_loaded, 16)
                sp.wait_ge(table_in, 16)
                sp.wait_ge(x_loaded, 64)

            @block.vector
            def _(dve):
                nc.vector.memset(neg_half, -0.5).then_inc(setup_done, 1)

        with nc.Fori(0, DEPTH) as layer:
            with nc.Block() as block:
                @block.tensor
                def _(pe):
                    mm, tr = nc.tensor.matmul, nc.tensor.transpose

                    def turn4(bank, parts, width=P):
                        for k, v in enumerate(parts):
                            last = tr(bank.t[0:width, k * P:(k + 1) * P], v, ident)
                        return last.then_inc(bank.full, 1)

                    def norm():
                        pe.wait_ge(params_in, 16 * 13)
                        pe.wait_ge(*room(mb[4], "colp"))
                        n = CONV * CB + KT
                        tr(mb[4].t[:, 0:n], rawp[0:n, :], ident[0:n, 0:n]).then_inc(mb[4].full, 1)
                        pe.wait_ge(*room(mb[5], "rpb"))
                        m = NAH * RPB_R
                        mm(mb[5].t[0:RPB_C, 0:NAH * 7], rpb[0:m, :], K("pick")[0:m, :], start=True, stop=True).then_inc(mb[5].full, 1)
                        for t in range(NT):
                            pe.wait_ge(h_ready, t + 1)
                            for q in range(2):
                                b = mb[2 * t + q]
                                pe.wait_ge(*room(b, ("hT", t, q)))
                                turn4(b, [xh[:, t, (4 * q + k) * P:(4 * q + k + 1) * P] for k in range(4)])

                    def gatecols():
                        pe.wait_ge(cols_in, 32)
                        pe.wait_ge(*released(("hT", 1, 1)))
                        pe.wait_ge(*room(mb[5], "gatecols"))
                        for t in range(NT):
                            for i, w in enumerate((w_ab, w_if)):
                                at = t * 32 + i * 16
                                for k in range(KT):
                                    last = mm(mb[5].t[:, at:at + 16], hT[:, k, t * P:(t + 1) * P], w[:, k, :], start=(k == 0), stop=(k == KT - 1))
                        last.then_inc(mb[5].full, 1)

                    def proj(kind, arg):
                        n = block_no[(kind, arg)]
                        w = ring[:, n % SLOTS].rearrange("p (k n) -> p k n", n=WB)
                        b = pj[pj_of[("proj", kind, arg)]]
                        if kind == "out" and arg == 0:
                            pe.wait_ge(*released(("mT", 1, 1)))
                        pe.wait_ge(ring_full[n % SLOTS], 16 * (n // SLOTS + 1))
                        pe.wait_ge(*room(b, ("pj", kind, arg)))
                        for i in range(2):
                            for k in range(KT):
                                o = b.t[:, i * WB:(i + 1) * WB]
                                if kind == "conv":
                                    last = mm(o, w[:, k, i * P:(i + 1) * P], hT[:, k, :], start=(k == 0), stop=(k == KT - 1))
                                else:
                                    last = mm(o, hT[:, k, i * P:(i + 1) * P], w[:, k, :], start=(k == 0), stop=(k == KT - 1))
                        last.then_inc(weights_used, 1)

                    def a_turn():
                        pe.wait_ge(silu_ready, 24)
                        for t in range(NT):
                            for q in range(3):
                                b = mb[(3 * t + q) % 4]
                                pe.wait_ge(*room(b, ("tm", t, q)))
                                turn4(b, [csl[:, 4 * q + k, t * P:(t + 1) * P] for k in range(4)])

                    def a_qkt():
                        for t in range(NT):
                            pe.wait_ge(normed_a, t + 1)
                            for q in range(2):
                                b = mb[2 * t + q]
                                pe.wait_ge(*room(b, ("qkt", t, q)))
                                turn4(b, [tm[:, t, (4 * q + k) * P:(4 * q + k + 1) * P] for k in range(4)])
                        for t in range(NT):
                            pe.wait_ge(*released(("qkt", t, 1)))
                            sl = slice(t * P, t * P + P)
                            for w in range(2):
                                b = mb[2 * t + w]
                                pe.wait_ge(*room(b, ("kkqk", t, w)))
                                for h in range(H):
                                    lhs = qkt[:, (H if w == 0 else 0) + h, sl]
                                    last = mm(b.t[:, h * P:(h + 1) * P], lhs, qkt[:, H + h, sl], start=True, stop=True)
                                last.then_inc(b.full, 1)

                    def cols():
                        pe.wait_ge(selected, 8)
                        pe.wait_ge(*room(mb[5], "cols"))
                        def gl(a, b):
                            return sel[:, a:b, 0:2, :].rearrange("p s k h -> p s (k h)")
                        o = mb[5].t[:, 0:P].rearrange("p (w s e) -> p w s e", w=4, s=STEPS)
                        for kind in range(2):
                            s0 = 2 * kind
                            mm(o[:, 0, s0:s0 + 2], K(f"cum{kind}"), gl(s0, s0 + 2), start=True, stop=True)
                            mm(o[:, 1, s0:s0 + 2], K(f"after{kind}"), gl(s0, s0 + 2), start=True, stop=True)
                        for half in range(2):
                            last = mm(o[:, 2 + half], K(f"half{half}"), gl(0, STEPS), start=True, stop=True)
                        last.then_inc(mb[5].full, 1)

                    def rows(s):
                        j = s % 2
                        pe.wait_ge(diag_ready, s + 1)
                        pe.wait_ge(*room(mb[j], ("gc", s)))
                        mm(mb[j].t[:, :], ones, prob[:, j].rearrange("p g n -> p (g n)"), start=True, stop=True).then_inc(mb[j].full, 1)

                    def solve0(s):
                        j = s % 2
                        pe.wait_ge(l_ready, s + 1)
                        pe.wait_ge(*room(mb[j], ("lt", s)))
                        turn4(mb[j], [lw[:, s, h] for h in range(H)])
                        pe.wait_ge(*room(mb[2 + j], ("qkdt", s)))
                        turn4(mb[2 + j], [qkd[:, s, h] for h in range(H)])

                    def product(bank, lhs, rhs):
                        for h in range(H):
                            last = mm(bank.t[:, h * P:(h + 1) * P], lhs[:, h], rhs[:, h], start=True, stop=True)
                        last.then_inc(bank.full, 1)

                    def t1(s, n):
                        j = s % 2
                        pe.wait_ge(lm_ready, solve_no(s, n) + 1)
                        if n == 1:
                            pe.wait_ge(x0_ready, 2 * s + 2)
                        else:
                            pe.wait_ge(*released(("dxt", s, n - 1)))
                        pe.wait_ge(*room(mb[j], ("t1", s, n)))
                        product(mb[j], sLm[:, j], sX[:, j])

                    def update(s, n):
                        j = s % 2
                        pe.wait_ge(*released(("t1", s, n)))
                        if n < LEVELS - 1:
                            pe.wait_ge(*room(mb[2 + j], ("dx", s, n)))
                            product(mb[2 + j], sXT[:, j], sT1[:, j])
                        pe.wait_ge(*room(mb[j], ("dxt", s, n)))
                        product(mb[j], sT1[:, j], sXT[:, j])

                    def uw(s):
                        j = s % 2
                        pe.wait_ge(*released(("dxt", s, LEVELS - 1)))
                        pe.wait_ge(scaled_uw, 4 * s + 2)
                        pe.wait_ge(*room(mb[j], ("u", s)))
                        product(mb[j], sXT[:, j], vk[:, 0])
                        pe.wait_ge(*room(mb[2 + j], ("w", s)))
                        product(mb[2 + j], vk[:, 1], sXT[:, j])
                        pe.wait_ge(scaled_uw, 4 * s + 3)
                        pe.wait_ge(*room(mb[j], ("qd", s)))
                        turn4(mb[j], [sLm[:, j, h] for h in range(H)])

                    def scan_v(s):
                        if s == 0:
                            return
                        pe.wait_ge(*released(("w", s)))
                        pe.wait_ge(*released(("kv", s - 1, 1)))
                        pe.wait_ge(*room(mb[0], ("ws", s)))
                        for h in range(H):
                            for half in range(2):
                                last = mm(mb[0].t[rows_of(half), h * P:(h + 1) * P], lw[:, s, h, rows_of(half)],
                                          st[:, half ^ KIND_OF[s], h], start=True, stop=True)
                        last.then_inc(mb[0].full, 1)

                    def scan_o(s):
                        j = s % 2
                        pe.wait_ge(*released(("qd", s)))
                        pe.wait_ge(*released(("qkdt", s)))
                        pe.wait_ge(*(released(("ws", s)) if s else (vn_ready, 1)))
                        pe.wait_ge(*room(mb[1], ("o", s)))
                        for h in range(H):
                            o = mb[1].t[:, h * P:(h + 1) * P]
                            if s > 0:
                                for half in range(2):
                                    mm(o[rows_of(half)], qdT[:, j, h, rows_of(half)], st[:, half ^ KIND_OF[s], h],
                                       start=True, stop=False, skip_group_check=True)
                            last = mm(o, qkd[:, s, h], vn[:, h], start=(s == 0), stop=True, skip_group_check=True)
                        last.then_inc(mb[1].full, 1)
                        if s == STEPS - 1:
                            return
                        pe.wait_ge(scaled_uw, 4 * s + 4)
                        for d in range(2):
                            b, r = mb[2 + d], rows_of(half_of(d, s))
                            pe.wait_ge(*room(b, ("kv", s, d)))
                            for h in range(H):
                                last = mm(b.t[:, h * P:(h + 1) * P], kd[r, j, h], vn[r, h], start=True, stop=True)
                            last.then_inc(b.full, 1)

                    def y_turn(name, t, bank, n):
                        pe.wait_ge(y_ready, y_no[(name + "_out", t)] + 1)
                        pe.wait_ge(*room(bank, ("y", name, t)))
                        turn4(bank, [y_tile[name][t][:, k * P:(k + 1) * P] for k in range(BK)])

                    def c_prep():
                        for t in range(NT):
                            pe.wait_ge(rotated, t + 1)
                            pe.wait_ge(*room(mb[4], ("cq", t)))
                            turn4(mb[4], [crp[:, t, k * P:(k + 1) * P] for k in range(4)])
                            pe.wait_ge(*room(mb[5], ("ck", t)))
                            turn4(mb[5], [crp[:, t, k * P:(k + 1) * P] for k in range(4, 6)])

                    def c_score(t, q):
                        pe.wait_ge(*released(("ck", 1)))
                        pe.wait_ge(*room(mb[4], ("cs", t, q)))
                        for m in range(2):
                            last = mm(mb[4].t[:, m * S:(m + 1) * S], cqT[:, 2 * q + m, t * P:(t + 1) * P], cqT[:, 4 + q, :], start=True, stop=True)
                        last.then_inc(mb[4].full, 1)

                    def c_turn(t, q):
                        pe.wait_ge(*released(("cs", t, q)))
                        pe.wait_ge(*room(mb[5], ("cp", t, q)))
                        turn4(mb[5], [prob[:, q, m, k * P:(k + 1) * P] for m in range(2) for k in range(NT)])

                    def c_mix(t, q):
                        pe.wait_ge(*released(("cp", t, q)))
                        pe.wait_ge(*room(mb[4], ("co", t, q)))
                        for m in range(2):
                            for k in range(NT):
                                last = mm(mb[4].t[:, m * P:(m + 1) * P], probT[:, m, k], ctm[:, k, 768 + q * HD:768 + (q + 1) * HD],
                                          start=(k == 0), stop=(k == NT - 1))
                        last.then_inc(mb[4].full, 1)

                    def b_bias(i):
                        b = mb[i % 2]
                        pe.wait_ge(*released("rpb"))
                        pe.wait_ge(*room(b, ("bias", i)))
                        z1 = K("toeplitz")[0:RPB_C]
                        for k in range(8):
                            c = 8 * i + k
                            last = mm(b.t[0:C, k * 56:(k + 1) * 56], z1[:, GRID - 1 - c:2 * GRID - 1 - c], rpbT[0:RPB_C, :], start=True, stop=True)
                        last.then_inc(b.full, 1)

                    def b_prep():
                        for t in range(NT):
                            for w in range(2):
                                pe.wait_ge(gained_b, 2 * t + w + 1)
                                pe.wait_ge(*room(mb[2 + w], ("nqk", t, w)))
                                turn4(mb[2 + w], [btm[:, t, w * BW + k * P:w * BW + (k + 1) * P] for k in range(4)])

                    def b_score(t, q):
                        pe.wait_ge(*released(("nqk", 1, 1)))
                        for par in range(2):
                            b, r = mb[par], rows_of(par)
                            pe.wait_ge(*room(b, ("bs", t, q, par)))
                            for m in range(2):
                                last = mm(b.t[:, m * S:(m + 1) * S], nqT[r, 2 * q + m, t * P:(t + 1) * P], nkT[r, 2 * q + m, :], start=True, stop=True)
                            last.then_inc(b.full, 1)

                    def b_turn(t, q):
                        for par in range(2):
                            pe.wait_ge(b_prob, 2 * group_no(t, q) + par + 1)
                            pe.wait_ge(*room(mb[2 + par], ("bp", t, q, par)))
                            turn4(mb[2 + par], [prob[:, par, m, k * P:(k + 1) * P] for m in range(2) for k in range(NT)])
                        pe.wait_ge(*room(mb[4], ("bo", t, q)))
                        for par in range(2):
                            pe.wait_ge(*released(("bp", t, q, par)))
                            for m in range(2):
                                i, h = 2 * m + par, 4 * q + 2 * m + par
                                for k in range(NT):
                                    last = mm(mb[4].t[:, i * NAD:(i + 1) * NAD], probTs[par][:, m, k], btm[:, k, 2 * BW + h * NAD:2 * BW + (h + 1) * NAD],
                                              start=(k == 0), stop=(k == NT - 1))
                        last.then_inc(mb[4].full, 1)

                    def d_prep():
                        for t in range(NT):
                            pe.wait_ge(*released(("pj", "d", 3)))
                            pe.wait_ge(*room(mb[t], ("mt", t)))
                            turn4(mb[t], [dtm[:, t, k * P:(k + 1) * P] for k in range(4)])
                        for t in range(NT):
                            pe.wait_ge(*released(("mt", t)))
                            for par in range(2):
                                b, r = mb[2 + par], rows_of(par)
                                pe.wait_ge(*room(b, ("mqk", t, par)))
                                for m in range(2):
                                    last = mm(b.t[:, m * P:(m + 1) * P], mqk_T[r, t, m], mqk_T[r, t, 2 + m], start=True, stop=True)
                                last.then_inc(b.full, 1)

                    def d_rows(s):
                        j = s % 2
                        pe.wait_ge(diag2_ready, s + 1)
                        pe.wait_ge(*room(mb[j], ("a", s)))
                        mm(mb[j].t[:, :], ones, prob[:, j].rearrange("p g n -> p (g n)"), start=True, stop=True).then_inc(mb[j].full, 1)

                    def d_step(s):
                        j = s % 2
                        pe.wait_ge(scaled_d, 2 * s + 1)
                        pe.wait_ge(*room(mb[2 + j], ("mqt", s)))
                        flat = mq[:, s].rearrange("p h n -> p (h n)")
                        turn4(mb[2 + j], [flat[:, k * P:(k + 1) * P] for k in range(2)])
                        pe.wait_ge(s_ready, s + 1)
                        pe.wait_ge(*room(mb[j], ("ms", s)))
                        turn4(mb[j], [mS[:, s, h] for h in range(H)])

                    def d_scan(s):
                        t, w = TILE_OF[s], HD + 1
                        pe.wait_ge(*released(("ms", s)))
                        pe.wait_ge(*released(("mqt", s)))
                        pe.wait_ge(ones_ready, 1)
                        if s > 0:
                            pe.wait_ge(*released(("mkv", s - 1, 1)))
                        for par in range(2):
                            b, r = mb[par], rows_of(par)
                            pe.wait_ge(*room(b, ("num", s, par)))
                            for m in range(2):
                                o = b.t[:, m * w:(m + 1) * w]
                                if s > 0:
                                    for half in range(2):
                                        mm(o[rows_of(half)], mqT[r, s, m, rows_of(half)], cst[r, half ^ KIND_OF[s], m],
                                           start=True, stop=False, skip_group_check=True)
                                last = mm(o, mS[:, s, 2 * m + par], vaug[:, t, 2 * m + par], start=(s == 0), stop=True, skip_group_check=True)
                            last.then_inc(b.full, 1)
                        if s == STEPS - 1:
                            return
                        pe.wait_ge(scaled_d, 2 * s + 2)
                        for d in range(2):
                            b, r = mb[2 + d], rows_of(half_of(d, s))
                            pe.wait_ge(*room(b, ("mkv", s, d)))
                            for m in range(2):
                                for par in range(2):
                                    last = mm(b.t[rows_of(par), m * w:(m + 1) * w], wk[r, s, 2 * m + par], vaug[r, t, 2 * m + par], start=True, stop=True)
                            last.then_inc(b.full, 1)

                    def branch(n, c):
                        k0 = block_no[("branch", (n, c))]
                        w = ring[:, k0 % SLOTS].rearrange("p (k n) -> p k n", n=512)
                        pe.wait_ge(*released(("y", "abcd"[n], 1)))
                        pe.wait_ge(ring_full[k0 % SLOTS], 16 * (k0 // SLOTS + 1))
                        first = pj_of[("branch", n, c)]
                        for t in range(NT):
                            b = pj[(first + t) % 2]
                            pe.wait_ge(*room(b, ("branch", n, c, t)))
                            for k in range(BK):
                                last = mm(b.t[:, :], yT[n][:, k, t * P:(t + 1) * P], w[:, k, :], start=(k == 0), stop=(k == BK - 1))
                        last.then_inc(weights_used, 1)

                    def merged_turn():
                        pe.wait_ge(merge_done, 12)
                        for t in range(NT):
                            for q in range(2):
                                b = mb[2 * t + q]
                                pe.wait_ge(*room(b, ("mT", t, q)))
                                turn4(b, [merged[:, q, t, k * P:(k + 1) * P] for k in range(4)])

                    run(norm=norm, gatecols=gatecols, proj=proj, a_turn=a_turn, a_qkt=a_qkt, cols=cols, rows=rows, solve0=solve0,
                        t1=t1, update=update, uw=uw, scan_v=scan_v, scan_o=scan_o,
                        a_out=lambda t: y_turn("a", t, mb[t], 0), c_out=lambda t: y_turn("c", t, mb[5], 2),
                        b_out=lambda t: y_turn("b", t, mb[5], 1), d_out=lambda t: y_turn("d", t, mb[4], 3),
                        c_prep=c_prep, c_score=c_score, c_turn=c_turn, c_mix=c_mix, b_bias=b_bias, b_prep=b_prep, b_score=b_score,
                        b_turn=b_turn, d_prep=d_prep, d_rows=d_rows, d_step=d_step, d_scan=d_scan, branch=branch, merged=merged_turn)

                @block.sync
                def _(sp):
                    sp.dma_start(w_ab[:, :, :], w_in[layer].rearrange("(k p) n -> p k n", p=P)[:, :, A_AB:A_AB + 16]).then_inc(cols_in, 16)
                    sp.dma_start(w_if[:, :, :], w_in[layer].rearrange("(k p) n -> p k n", p=P)[:, :, D_IF:D_IF + 16]).then_inc(cols_in, 16)
                    sp.dma_start(rawp[0:CONV * CB, :], conv_a[layer].rearrange("j (b c) -> (j b) c", c=P)).then_inc(params_in, 16)
                    sp.dma_start(rawp[CONV * CB:CONV * CB + KT, :], norm_g[layer].rearrange("(k c) -> k c", c=P)).then_inc(params_in, 16)
                    sp.dma_start(rpb[0:NAH * RPB_R, :], na_rpb[layer].rearrange("h r c -> (h r) c")).then_inc(params_in, 16)
                    shared = [(g_dn, dn_norm_g[layer]), (g_ml, ml_norm_g[layer]), (g_nq, na_q_norm[layer]), (g_nk, na_k_norm[layer]),
                              (graw[:, 0], ga_q_norm[layer]), (graw[:, 2], ga_k_norm[layer])]
                    for dst, src in shared:
                        sp.dma_start(dst, src[None, :].to_broadcast([P, src.shape[0]])).then_inc(params_in, 16)
                    for k, src in enumerate((dn_dt_bias, ml_f_bias, dn_a_log, ml_i_bias)):
                        src = src[layer].rearrange("d h -> (d h)")
                        sp.dma_start(g_gate[:, k], src[None, :].to_broadcast([P, 8])).then_inc(params_in, 16)

                    sources = {"branch": lambda a: w_branch[layer, a[0]], "out": lambda a: w_out[layer]}
                    for n, (kind, arg, col) in enumerate(plan):
                        if n >= SLOTS:
                            sp.wait_ge(weights_used, n - SLOTS + 1)
                        width = 512 if kind == "branch" else WB
                        src = sources.get(kind, lambda a: w_in[layer])(arg).rearrange("(k p) n -> p k n", p=P)
                        sp.dma_start(ring[:, n % SLOTS].rearrange("p (k n) -> p k n", n=width), src[:, :, col:col + width])\
                          .then_inc(ring_full[n % SLOTS], 16)

                @block.scalar
                def _(act):
                    copy, f = nc.scalar.activation, nc.scalar.activation

                    def take(key, dst, view, scale=1.0):
                        act.wait_ge(*filled(key))
                        f(dst, view(bank_of(key).t), ACT.Copy, scale=scale).then_inc(bank_of(key).free, 1)

                    def four(t):
                        return t.rearrange("p (k n) -> p k n", k=4)

                    def two(t):
                        return t.rearrange("p (k n) -> p k n", k=2)

                    def norm():
                        act.wait_ge(*filled("colp"))
                        f(colp, mb[4].t[:, 0:CONV * CB + KT], ACT.Copy).then_inc(mb[4].free, 1)
                        act.wait_ge(*filled("rpb"))
                        f(rpbT[0:RPB_C], mb[5].t[0:RPB_C, 0:NAH * 7], ACT.Copy).then_inc(mb[5].free, 1)

                    def x_squares():
                        for t in range(NT):
                            f(xh[:, t], x[:, t], ACT.Square, accum_out=ssx[:, t:t + 1]).then_inc(x_squared, 1)

                    def proj(kind, arg):
                        key = ("pj", kind, arg)
                        b = bank_of(key)
                        if kind == "out":
                            return
                        act.wait_ge(weights_used, block_no[(kind, arg)] + 1)
                        if kind == "conv":
                            src = b.t.rearrange("p (b c n) -> p b c n", b=2, c=STEPS)
                            dst = cin[:, 2 * arg:2 * arg + 2, 2:2 + S].rearrange("p b (c n) -> p b c n", c=STEPS)
                            f(dst[:, :, 0:4:3], src[:, :, 0:2], ACT.Copy)
                            f(dst[:, :, 1:3], src[:, :, 2:4], ACT.Copy).then_inc(b.free, 1)
                            return
                        cols = slice(arg * WB, (arg + 1) * WB) if kind != "gate" else slice(arg[2] * WB, (arg[2] + 1) * WB)
                        if kind[0] == "z":
                            f(z["abcd".index(kind[1])][:, :, cols], two(b.t), ACT.Tanh, scale=0.5).then_inc(z_tanh, 1)
                        elif kind == "o":
                            if arg == 0:
                                act.wait_ge(*released(("y", "c", 1)))
                            f(og[:, :, cols], two(b.t), ACT.Tanh, scale=0.5).then_inc(b.free, 1)
                        elif kind == "gate":
                            i = branch_no[arg[:2]]
                            if i >= 2:
                                n, c = branch_list[i - 2]
                                act.wait_ge(*released(("branch", n, c, 1)))
                                if n != BRANCHES[0]:
                                    act.wait_ge(merge_done, NT * (i - 4) + 2)
                            f(gact[i % 2][:, :, cols], two(b.t), ACT.Tanh, scale=0.5).then_inc(b.free, 1)
                        elif kind == "c":
                            if arg == 0:
                                act.wait_ge(*released(("hT", 1, 1)))
                            take_pj(b, ctm[:, :, cols], two(b.t))
                        elif kind == "b":
                            take_pj(b, btm[:, :, cols], two(b.t))
                        elif arg < 2:
                            if arg == 0:
                                act.wait_ge(*released(("y", "c", 1)))
                            take_pj(b, dtm[:, :, cols], two(b.t))
                        else:
                            h = 2 * (arg - 2)
                            take_pj(b, vaug[:, :, h:h + 2, 0:HD], b.t.rearrange("p (t h n) -> p t h n", t=NT, h=2))

                    def take_pj(b, dst, src):
                        f(dst, src, ACT.Copy).then_inc(b.free, 1)

                    def gatecols():
                        act.wait_ge(*released("gatecols"))
                        f(raw[:, :, 2], gps[:, :, 8:16], ACT.Tanh, scale=0.5).then_inc(gate_exp, 1)
                        act.wait_ge(params_in, 16 * 13)
                        f(coef[:, 0], g_gate[:, 2], ACT.Exp).then_inc(gate_exp, 1)
                        act.wait_ge(softplus_in, 1)
                        f(softp, softp, ACT.Exp).then_inc(gate_exp, 1)
                        act.wait_ge(gate_exp, 3)
                        f(softp, softp, ACT.Ln, bias=1.0).then_inc(gate_exp, 1)

                    def conv(i):
                        act.wait_ge(conv_out, 2 * i + 2)
                        f(cin[:, 2 * i:2 * i + 2, 0:S], cac[:, 2 * i:2 * i + 2], ACT.Tanh, scale=0.5).then_inc(conv_act, 1)

                    def cols():
                        act.wait_ge(*filled("cols"))
                        flat = "p w s e -> p (w s e)"
                        f(cc.rearrange(flat), mb[5].t[:, 0:P], ACT.Copy).then_inc(mb[5].free, 1)
                        act.wait_ge(*released("cols"))
                        f(ex.rearrange(flat), cc.rearrange(flat), ACT.Exp).then_inc(sums_ready, 1)

                    def a_turn():
                        for t in range(NT):
                            for q in range(3):
                                take(("tm", t, q), tm[:, t, q * 512:(q + 1) * 512], lambda b: b)

                    def a_norm():
                        for t in range(NT):
                            act.wait_ge(*released(("tm", t, 1)))
                            sq = st.rearrange("p d h n -> p (d h n)")
                            if t:
                                act.wait_ge(summed_a, 1)
                            f(sq, tm[:, t, 0:1024], ACT.Square).then_inc(squared_a, 1)

                    def a_qkt():
                        for t in range(NT):
                            for q in range(2):
                                take(("qkt", t, q), qkt[:, 4 * q:4 * q + 4, t * P:(t + 1) * P], four)
                        for t in range(NT):
                            for w in range(2):
                                take(("kkqk", t, w), kkqk[:, t, w], four)

                    def rows(s):
                        act.wait_ge(decay_arg, s + 1)
                        f(st[:, s % 2], st[:, s % 2], ACT.Exp, scale=-1.0).then_inc(decay_ready, 1)

                    def solve0(s):
                        j = s % 2
                        if s >= 2:
                            act.wait_ge(lm_ready, solve_no(s - 2, LEVELS - 1) + 1)
                        take(("lt", s), sLT[:, j], four)
                        take(("qkdt", s), qkd[:, s], four)

                    def t1(s, n):
                        take(("t1", s, n), sT1[:, s % 2], four)

                    def uw(s):
                        take(("u", s), us[:, s], four)
                        take(("w", s), lw[:, s], four)
                        take(("qd", s), qdT[:, s % 2], four)

                    def scan_o(s):
                        take(("o", s), us[:, s], four)

                    def a_sum(t):
                        act.wait_ge(y_in, sum_no[("a_sum", t)] + 1)
                        f(o_sq["a"][t], o_sum["a"][t], ACT.Square).then_inc(squared_y, 1)

                    def d_sum(t):
                        act.wait_ge(y_in, sum_no[("d_sum", t)] + 1)
                        f(o_sq["d"][t], o_sum["d"][t], ACT.Square).then_inc(squared_y, 1)

                    def y_out(name, t):
                        take(("y", name, t), yT["abcd".index(name)][:, :, t * P:(t + 1) * P], four)

                    def c_prep():
                        act.wait_ge(*released(("pj", "c", 3)))
                        f(crp[:, :, :], ctm[:, :, 0:768], ACT.Square).then_inc(squared_c, 1)
                        for t in range(NT):
                            take(("cq", t), cqT[:, 0:4, t * P:(t + 1) * P], four)
                            take(("ck", t), cqT[:, 4:6, t * P:(t + 1) * P], lambda b: two(b[:, 0:256]))

                    def c_score(t, q):
                        act.wait_ge(c_max, group_no(t, q) + 1)
                        b = bank_of(("cs", t, q))
                        if group_no(t, q) >= 2:
                            act.wait_ge(*filled(("cp", t - 1, q)))
                        for m in range(2):
                            h = 2 * q + m
                            last = f(prob[:, q, m], b.t[:, m * S:(m + 1) * S], ACT.Exp, scale=HD ** -0.5, bias=nmc[:, t, h:h + 1],
                                     accum_out=smc[:, t, h:h + 1])
                        last.then_inc(b.free, 1)

                    def c_turn(t, q):
                        if group_no(t, q) >= 1:
                            act.wait_ge(*filled(("co", (group_no(t, q) - 1) // 2, 1 - q)))
                        take(("cp", t, q), probT.rearrange("p g k n -> p (g k n)"), lambda b: b)

                    def b_prep():
                        act.wait_ge(*released(("bias", 7)))
                        for t in range(NT):
                            sq = (mq if t == 0 else wk).rearrange("p s h n -> p (s h n)")
                            f(sq, btm[:, t, 0:1024], ACT.Square).then_inc(squared_b, 1)
                        for t in range(NT):
                            for w in range(2):
                                take(("nqk", t, w), (nqT, nkT)[w][:, :, t * P:(t + 1) * P], four)

                    def b_score(t, q):
                        for par in range(2):
                            act.wait_ge(b_max, 2 * group_no(t, q) + par + 1)
                            for m in range(2):
                                h = 4 * q + 2 * m + par
                                last = f(prob[:, par, m], prob[:, par, m], ACT.Exp, bias=nmb[:, t, h:h + 1], accum_out=smb[:, t, h:h + 1])
                            last.then_inc(b_prob, 1)

                    def b_turn(t, q):
                        for par in range(2):
                            if group_no(t, q) >= 1:
                                n = group_no(t, q) - 1
                                act.wait_ge(*filled(("bo", n // 2, n % 2)))
                            take(("bp", t, q, par), probTs[par].rearrange("p g k n -> p (g k n)"), lambda b: b)

                    def d_prep():
                        for t in range(NT):
                            take(("mt", t), mqk_T[:, t], four)
                        for t in range(NT):
                            for par in range(2):
                                take(("mqk", t, par), mqk[:, t, par:H:2], lambda b: two(b[:, 0:256]), scale=MLK ** -0.5)

                    def d_m():
                        act.wait_ge(m_args, 4)
                        f(e_out.rearrange("p k s h -> p (k s h)"), e_in.rearrange("p k s h -> p (k s h)"), ACT.Exp).then_inc(m_exp, 1)
                        f(dec.rearrange("p s k h -> p (s k h)"), dec_in.rearrange("p s k h -> p (s k h)"), ACT.Exp).then_inc(m_exp, 1)

                    def d_step(s):
                        act.wait_ge(s_arg, s + 1)
                        f(mS[:, s], mS[:, s], ACT.Exp).then_inc(s_exp, 1)
                        take(("mqt", s), mqT[:, s], lambda b: two(b[:, 0:256]))
                        take(("ms", s), mS[:, s], four)

                    def d_scan(s):
                        w = HD + 1
                        for par in range(2):
                            take(("num", s, par), num[:, s, par:H:2], lambda b: two(b[:, 0:2 * w]))

                    def merged_turn():
                        for t in range(NT):
                            for q in range(2):
                                take(("mT", t, q), hT[:, 4 * q:4 * q + 4, t * P:(t + 1) * P], four, scale=0.5)

                    x_squares()
                    run(norm=norm, proj=proj, gatecols=gatecols, conv=conv, cols=cols, a_turn=a_turn, a_norm=a_norm, a_qkt=a_qkt,
                        rows=rows, solve0=solve0, t1=t1, uw=uw, scan_o=scan_o, a_sum=a_sum, d_sum=d_sum,
                        a_out=lambda t: y_out("a", t), b_out=lambda t: y_out("b", t), c_out=lambda t: y_out("c", t),
                        d_out=lambda t: y_out("d", t), c_prep=c_prep, c_score=c_score, c_turn=c_turn, b_prep=b_prep,
                        b_score=b_score, b_turn=b_turn, d_prep=d_prep, d_m=d_m, d_step=d_step, d_scan=d_scan, merged=merged_turn)

                @block.vector
                def _(dve):
                    tt, ts, stt, reduce = nc.vector.tensor_tensor, nc.vector.tensor_scalar, nc.vector.scalar_tensor_tensor, nc.vector.tensor_reduce
                    chain = [0]

                    def mark(ins):
                        chain[0] += 1
                        ins.then_inc(dve_chain, 1)
                        return chain[0]

                    def link(ins):
                        dve.wait_ge(dve_chain, mark(ins))

                    def four(t):
                        return t.rearrange("p (k n) -> p k n", k=4)

                    def two(t):
                        return t.rearrange("p (k n) -> p k n", k=2)

                    def flat(v):
                        return v.rearrange("p h n -> p (h n)")

                    def norm():
                        mark(nc.vector.memset(cin[:, :, 0:2], 0.0))
                        link(nc.vector.memset(cin[:, :, 2 + S:4 + S], 0.0))
                        dve.wait_ge(rms_x, 1)
                        for t in range(NT):
                            ts(xh[:, t], x[:, t], rsx[:, t:t + 1], None, ALU.mult).then_inc(h_ready, 1)
                        dve.wait_ge(*released("colp"))
                        for t in range(NT):
                            for q in range(2):
                                dve.wait_ge(*filled(("hT", t, q)))
                                b = bank_of(("hT", t, q))
                                k0 = CONV * CB + 4 * q
                                tt(hT[:, 4 * q:4 * q + 4, t * P:(t + 1) * P], four(b.t), along(colp[:, k0:k0 + 4], P), ALU.mult).then_inc(b.free, 1)

                    def gatecols():
                        b = mb[5]
                        dve.wait_ge(*filled("gatecols"))
                        nc.vector.tensor_copy(gps.rearrange("p t e -> p (t e)"), b.t[:, 0:64]).then_inc(b.free, 1)
                        dve.wait_ge(*released("gatecols"))
                        dve.wait_ge(params_in, 16 * 13)
                        tt(raw[:, :, 0], gps[:, :, 0:8], over(g_gate[:, 0], NT), ALU.add)
                        stt(raw[:, :, 1], gps[:, :, 24:32], -1.0, over(g_gate[:, 1], NT), ALU.mult, ALU.subtract)
                        link(tt(raw[:, :, 3], gps[:, :, 16:24], over(g_gate[:, 3], NT), ALU.add))
                        for k in range(2):
                            last = stt(softp[:, :, k], raw[:, :, k], -1.0, raw[:, :, k], ALU.mult, ALU.min)
                            if k == 0:
                                link(last)
                        last.then_inc(softplus_in, 1)
                        dve.wait_ge(gate_exp, 2)
                        ts(coef[:, 0], coef[:, 0], -1.0, None, ALU.mult)
                        nc.vector.memset(coef[:, 1], -1.0)
                        link(ts(raw[:, :, 2], raw[:, :, 2], 0.5, 0.5, ALU.mult, ALU.add))
                        dve.wait_ge(gate_exp, 4)
                        for k in range(2):
                            link(stt(softp[:, :, k], raw[:, :, k], 0.0, softp[:, :, k], ALU.max, ALU.add))
                        for k in range(2):
                            tt(raw[:, :, k], softp[:, :, k], over(coef[:, k], NT), ALU.mult).then_inc(gates_ready, 1)

                    def conv(i):
                        dve.wait_ge(*released(("pj", "conv", i)))
                        done = [0, 0]
                        for j in range(CONV):
                            for m in range(2):
                                b = 2 * i + m
                                w = colp[:, j * CB + b:j * CB + b + 1]
                                if j == 0:
                                    done[m] = mark(ts(cac[:, b], cin[:, b, 0:S], w, None, ALU.mult))
                                    continue
                                dve.wait_ge(dve_chain, done[m])
                                last = stt(cac[:, b], cin[:, b, j:j + S], w, cac[:, b], ALU.mult, ALU.add)
                                if j < CONV - 1:
                                    done[m] = mark(last)
                                else:
                                    last.then_inc(conv_out, 1)
                        if i > 0:
                            silu(i - 1)
                        if i == 5:
                            silu(i)

                    def silu(i):
                        dve.wait_ge(conv_act, i + 1)
                        for b in range(2 * i, 2 * i + 2):
                            a = cin[:, b, 0:S].rearrange("p (c n) -> p c n", c=STEPS)
                            v = cac[:, b].rearrange("p (c n) -> p c n", c=STEPS)
                            o = csl[:, b].rearrange("p (c n) -> p c n", c=STEPS)
                            for t, sl in ((0, slice(0, 4, 3)), (1, slice(1, 3))):
                                stt(o[:, 2 * t:2 * t + 2], a[:, sl], 1.0, v[:, sl], ALU.add, ALU.mult).then_inc(silu_ready, 1)

                    def cols():
                        dve.wait_ge(selected, 8)
                        dve.wait_ge(sums_ready, 1)
                        ts(hbeta, sel[:, :, 2], 0.5, None, ALU.mult).then_inc(terms_ready, 1)
                        tt(bev, sel[:, :, 2], ex[:, 0, :, 0:H], ALU.mult).then_inc(terms_ready, 1)
                        tt(av, sel[:, :, 3], cc[:, 0, :, H:8], ALU.subtract).then_inc(terms_ready, 1)

                    def a_norm():
                        sq = st.rearrange("p d h n -> p (d h) n")
                        for t in range(NT):
                            dve.wait_ge(squared_a, t + 1)
                            reduce(ssa[:, t], sq, X, ALU.add).then_inc(summed_a, 1)
                        dve.wait_ge(rms_a, 2)
                        for t in range(NT):
                            v = tm[:, t, 0:1024].rearrange("p (g n) -> p g n", g=8)
                            tt(v, v, along(rsa[:, t], P), ALU.mult).then_inc(normed_a, 1)

                    def rows(s):
                        j, kind, t = s % 2, KIND_OF[s], TILE_OF[s]
                        dve.wait_ge(*filled(("gc", s)))
                        b = bank_of(("gc", s))
                        if s == 0:
                            dve.wait_ge(*released(("kkqk", 1, 1)))
                        if s >= 2:
                            dve.wait_ge(decay_beta, s - 1)
                        tt(st[:, j], four(b.t), along(cc[:, 0, s, 0:H], P), ALU.subtract).then_inc(b.free, 1)
                        dve.wait_ge(*released(("gc", s)))
                        stt(st[:, j], st[:, j], 0.0, over(K(f"mask{kind}"), H), ALU.max, ALU.subtract).then_inc(decay_arg, 1)
                        dve.wait_ge(decay_ready, s + 1)
                        tt(qkd[:, s], st[:, j], kkqk[:, t, 1], ALU.mult)
                        dve.wait_ge(decay_beta, s + 1)
                        tt(lw[:, s], vk[:, j], kkqk[:, t, 0], ALU.mult).then_inc(l_ready, 1)

                    def update(s, n):
                        j = s % 2
                        if n < LEVELS - 1:
                            b = bank_of(("dx", s, n))
                            dve.wait_ge(*filled(("dx", s, n)))
                            tt(sX[:, j], sX[:, j], four(b.t), ALU.subtract).then_inc(b.free, 1)
                        b = bank_of(("dxt", s, n))
                        dve.wait_ge(*filled(("dxt", s, n)))
                        tt(sXT[:, j], sXT[:, j], four(b.t), ALU.subtract).then_inc(b.free, 1)

                    def scan_v(s):
                        dve.wait_ge(*released(("u", s)))
                        if s == 0:
                            nc.vector.tensor_copy(vn, us[:, 0]).then_inc(vn_ready, 1)
                            return
                        dve.wait_ge(*filled(("ws", s)))
                        tt(vn, us[:, s], four(mb[0].t), ALU.subtract).then_inc(mb[0].free, 1)

                    def scan_o(s):
                        if s == STEPS - 1:
                            return
                        for d in range(2):
                            b = mb[2 + d]
                            dve.wait_ge(*filled(("kv", s, d)))
                            if s == 0:
                                nc.vector.tensor_copy(st[:, d], four(b.t)).then_inc(b.free, 1)
                            else:
                                dve.wait_ge(st_decayed, 2 * (s - 1) + d + 1)
                                tt(st[:, d], st[:, d], four(b.t), ALU.add).then_inc(b.free, 1)

                    def sum_square(name, t, a, b):
                        n = sum_no[(name + "_sum", t)]
                        tt(o_sum[name][t], a, b, ALU.add).then_inc(y_in, 1)
                        dve.wait_ge(squared_y, n + 1)
                        reduce(sso[:, t + (2 if name == "d" else 0)], o_sq[name][t], X, ALU.add).then_inc(summed_y, 1)

                    def a_sum(t):
                        dve.wait_ge(*released(("o", STEPS - 1)))
                        sum_square("a", t, *((us[:, 0], us[:, 3]) if t == 0 else (us[:, 1], us[:, 2])))

                    def norm_gate(name, t, gain, factor):
                        n = sum_no[(name + "_sum", t)]
                        o = o_sum[name][t]
                        dve.wait_ge(rms_y, n + 1)
                        link(tt(o, o, along(rso[:, t + (2 if name == "d" else 0)], HD), ALU.mult))
                        link(tt(o, o, over(gain, H), ALU.mult))
                        gate_y(name, t, factor)

                    def gate_y(name, t, factor):
                        y = y_tile[name][t]
                        stt(y, y, factor, z["abcd".index(name)][:, t], ALU.mult, ALU.mult).then_inc(y_ready, 1)

                    def a_out(t):
                        norm_gate("a", t, g_dn, 0.5)

                    def d_out(t):
                        norm_gate("d", t, g_ml, 0.25)

                    def z_gate(kind, i):
                        b = bank_of(("pj", kind, i))
                        dve.wait_ge(z_tanh, z_no[(kind, i)] + 1)
                        v = z["abcd".index(kind[1])][:, :, i * WB:(i + 1) * WB]
                        stt(v, v, 1.0, two(b.t), ALU.add, ALU.mult).then_inc(b.free, 1)

                    def proj(kind, arg):
                        if kind[0] == "z":
                            z_gate(kind, arg)
                        if kind == "out":
                            b = bank_of(("pj", kind, arg))
                            dve.wait_ge(weights_used, block_no[(kind, arg)] + 1)
                            v = x[:, :, arg * WB:(arg + 1) * WB]
                            tt(v, v, two(b.t), ALU.add).then_inc(b.free, 1)

                    def c_prep():
                        dve.wait_ge(squared_c, 1)
                        reduce(ssc.rearrange("p t g -> p (t g)"), crp.rearrange("p t (g n) -> p t g n", g=6), X, ALU.add).then_inc(summed_c, 1)
                        dve.wait_ge(summed_c, 1)
                        dve.wait_ge(rope_ready, 4)
                        for t in range(NT):
                            swp = prob.rearrange("p j g n -> p (j g n)")[:, 0:768]
                            for h0, h1, w in ((0, 4, 0), (4, 6, 2)):
                                src = ctm[:, t, h0 * HD:h1 * HD]
                                out_ = crp[:, t, h0 * HD:h1 * HD]
                                tt(heads(out_, h1 - h0), heads(src, h1 - h0), over(rope[:, w, t], h1 - h0), ALU.mult)
                                sv = src.rearrange("p (h s n) -> p h s n", s=2, n=32)
                                dv = swp[:, h0 * HD:h1 * HD].rearrange("p (h s n) -> p h s n", s=2, n=32)
                                rv = rope[:, w + 1, t].rearrange("p (a s n) -> p a s n", a=2, s=2)
                                for a in range(2):
                                    for s in range(2):
                                        sl = slice(a, 2 * (h1 - h0), 2)
                                        last = mark(tt(dv[:, sl, s], sv[:, sl, 1 - s], over(rv[:, a, s], h1 - h0), ALU.mult))
                            dve.wait_ge(dve_chain, last)
                            link(tt(crp[:, t], crp[:, t], swp, ALU.add))
                            if t == 0:
                                dve.wait_ge(rms_c, 1)
                            tt(heads(crp[:, t], 6), heads(crp[:, t], 6), along(rsc[:, t], HD), ALU.mult).then_inc(rotated, 1)

                    def c_score(t, q):
                        b = bank_of(("cs", t, q))
                        dve.wait_ge(*filled(("cs", t, q)))
                        m = nmc[:, t, 2 * q:2 * q + 2]
                        link(reduce(m, two(b.t), X, ALU.max, negate=True))
                        ts(m, m, HD ** -0.5, None, ALU.mult).then_inc(c_max, 1)

                    def c_mix(t, q):
                        b = bank_of(("co", t, q))
                        link(nc.vector.reciprocal(rmc[:, t, 2 * q:2 * q + 2], smc[:, t, 2 * q:2 * q + 2]))
                        dve.wait_ge(*filled(("co", t, q)))
                        tt(heads(crp[:, t, q * 256:(q + 1) * 256], 2), two(b.t[:, 0:256]), along(rmc[:, t, 2 * q:2 * q + 2], HD), ALU.mult)\
                            .then_inc(b.free, 1)

                    def c_sum(t):
                        dve.wait_ge(*released(("co", t, 1)))
                        gate_y("c", t, 0.5)

                    def b_sum(t):
                        dve.wait_ge(*released(("bo", t, 1)))
                        gate_y("b", t, 0.5)

                    def b_bias(i):
                        if i == 0:
                            dve.wait_ge(*released(("y", "a", 1)))
                        dve.wait_ge(*filled(("bias", i)))
                        b = bank_of(("bias", i))
                        src = b.t[0:C, 0:8 * 56].rearrange("p (c h o) -> p h o c", c=8, h=NAH)
                        for t in range(NT):
                            for half in range(2):
                                r = CHUNKS[t][half]
                                dst = bias[rows_of(half), t].rearrange("p h (k c) -> p h k c", k=STEPS)[:, :, :, 8 * i:8 * i + 8]
                                win = K("window")[0:C, 8 * i:8 * i + 8][:, None, None, :].to_broadcast([C, NAH, 2, 8])
                                tt(dst[:, :, 0:2], src[:, :, 3 - r:7 - r:3], win, ALU.add)
                                last = tt(dst[:, :, 2:4], src[:, :, 4 - r:6 - r], win, ALU.add)
                        last.then_inc(b.free, 1)

                    def b_prep():
                        for t in range(NT):
                            dve.wait_ge(squared_b, t + 1)
                            sq = (mq if t == 0 else wk).rearrange("p s h n -> p (s h) n")
                            reduce(ssb[:, t], sq, X, ALU.add).then_inc(summed_b, 1)
                        dve.wait_ge(rms_b, 1)
                        for t in range(NT):
                            v = btm[:, t, 0:1024].rearrange("p (g n) -> p g n", g=16)
                            tt(v, v, along(rsb[:, t], NAD), ALU.mult).then_inc(scaled_b, 1)

                    def b_score(t, q):
                        for par in range(2):
                            b = bank_of(("bs", t, q, par))
                            dve.wait_ge(*filled(("bs", t, q, par)))
                            n = group_no(t, q)
                            if n >= 1:
                                dve.wait_ge(*filled(("bp", (n - 1) // 2, (n - 1) % 2, par)))
                            hs = slice(4 * q + par, 4 * q + par + 3, 2)
                            stt(prob[:, par], two(b.t), NAD ** -0.5, bias[:, t, hs], ALU.mult, ALU.add).then_inc(b.free, 1)
                            dve.wait_ge(*released(("bs", t, q, par)))
                            reduce(nmb[:, t, hs], prob[:, par], X, ALU.max, negate=True).then_inc(b_max, 1)

                    def b_turn(t, q):
                        b = bank_of(("bo", t, q))
                        dve.wait_ge(b_prob, 2 * group_no(t, q) + 2)
                        link(nc.vector.reciprocal(rmb[:, t, 4 * q:4 * q + 4], smb[:, t, 4 * q:4 * q + 4]))
                        dve.wait_ge(*filled(("bo", t, q)))
                        tt(btm[:, t, q * 256:(q + 1) * 256].rearrange("p (h n) -> p h n", h=4), four(b.t[:, 0:256]),
                           along(rmb[:, t, 4 * q:4 * q + 4], NAD), ALU.mult).then_inc(b.free, 1)

                    def d_prep():
                        dve.wait_ge(*released(("pj", "o", 1)))
                        dve.wait_ge(*released(("pj", "zd", 1)))
                        for t in range(NT):
                            mark(stt(z[3][:, t], og[:, t], 1.0, z[3][:, t], ALU.add, ALU.mult))

                    def d_rows(s):
                        b = bank_of(("a", s))
                        dve.wait_ge(*filled(("a", s)))
                        link(tt(mS[:, s], four(b.t), over(K(f"mask{KIND_OF[s]}"), H), ALU.add))
                        reduce(amx[:, s], b.t.rearrange("p (h k n) -> p h k n", h=H, k=2), X, ALU.max).then_inc(b.free, 1)
                        mark(reduce(cm[:, s], mS[:, s], X, ALU.max))

                    def d_m():
                        link(nc.vector.memset(mst[:, 0], 0.0))
                        for s in range(STEPS):
                            link(tt(mxs[:, s], mst[:, s], amx[:, s].rearrange("p h k -> p k h"), ALU.max))
                            if s == STEPS - 1:
                                break
                            swap = KIND_OF[s] != KIND_OF[s + 1]
                            for k in range(2):
                                link(tt(mst[:, s + 1, k ^ swap], cc[:, 2 + k, s, H:8], mxs[:, s, k], ALU.add))
                        for half in range(2):
                            r = rows_of(half)
                            nc.vector.tensor_copy(msel[r], mst[r, :, half])
                            link(nc.vector.tensor_copy(mxsel[r], mxs[r, :, half]))
                        link(tt(mrun, cm, msel, ALU.max))
                        tt(e_in[:, 0], msel, mrun, ALU.subtract).then_inc(m_args, 1)
                        stt(e_in[:, 1], cc[:, 0, :, H:8], -1.0, mrun, ALU.mult, ALU.subtract).then_inc(m_args, 1)
                        tt(e_in[:, 2], av, mxsel, ALU.subtract).then_inc(m_args, 1)
                        tt(dec_in, mst, mxs, ALU.subtract).then_inc(m_args, 1)
                        dve.wait_ge(m_exp, 2)
                        ts(e_out[:, 2], e_out[:, 2], MLK ** -0.5, None, ALU.mult).then_inc(m_terms, 1)

                    def d_step(s):
                        tt(mS[:, s], mS[:, s], along(mrun[:, s], P), ALU.subtract).then_inc(s_arg, 1)
                        dve.wait_ge(s_exp, s + 1)
                        dve.wait_ge(*released(("mqk", 1, 1)))
                        tt(mS[:, s], mS[:, s], mqk[:, TILE_OF[s]], ALU.mult).then_inc(s_ready, 1)

                    def d_scan(s):
                        if s == STEPS - 1:
                            return
                        for d in range(2):
                            b = mb[2 + d]
                            v = two(b.t[:, 0:2 * (HD + 1)])
                            dve.wait_ge(*filled(("mkv", s, d)))
                            if s == 0:
                                nc.vector.tensor_copy(cst[:, d], v).then_inc(b.free, 1)
                            else:
                                dve.wait_ge(c_decayed, 2 * (s - 1) + d + 1)
                                tt(cst[:, d], cst[:, d], v, ALU.add).then_inc(b.free, 1)

                    def d_den():
                        dve.wait_ge(*released(("num", STEPS - 1, 1)))
                        v = num[:, :, :, HD]
                        link(stt(nden, v, -1.0, v, ALU.mult, ALU.max))
                        link(tt(nden, nden, e_out[:, 1], ALU.max))
                        link(nc.vector.reciprocal(den, nden))
                        for s in range(STEPS):
                            o = num[:, s, :, 0:HD]
                            last = mark(tt(o, o, along(den[:, s], HD), ALU.mult))
                        dve.wait_ge(dve_chain, last)

                    def d_sum(t):
                        a, b = (0, 3) if t == 0 else (1, 2)
                        sum_square("d", t, num[:, a, :, 0:HD], num[:, b, :, 0:HD])

                    def branch(n, c):
                        i = branch_no[(n, c)]
                        k = block_no[("branch", (n, c))]
                        dve.wait_ge(weights_used, k + 1)
                        dve.wait_ge(*released(("pj", "gate", (n, c, 1))))
                        for t in range(NT):
                            b = bank_of(("branch", n, c, t))
                            dst = merged[:, c, t] if n == BRANCHES[0] else gact[i % 2][:, t]
                            stt(dst, gact[i % 2][:, t], 1.0, b.t, ALU.add, ALU.mult).then_inc(b.free, 1)

                    run(norm=norm, gatecols=gatecols, conv=conv, cols=cols, a_norm=a_norm, rows=rows, update=update, scan_v=scan_v,
                        scan_o=scan_o, a_sum=a_sum, a_out=a_out, d_out=d_out, proj=proj, c_prep=c_prep, c_score=c_score, c_mix=c_mix,
                        c_sum=c_sum, b_sum=b_sum, b_bias=b_bias, b_prep=b_prep, b_score=b_score, b_turn=b_turn, d_prep=d_prep,
                        d_rows=d_rows, d_m=d_m, d_step=d_step, d_scan=d_scan, d_den=d_den, d_sum=d_sum, branch=branch)

                @block.gpsimd
                def _(pool):
                    chain = [0]

                    def link(ins):
                        chain[0] += 1
                        ins.then_inc(pool_chain, 1)
                        pool.wait_ge(pool_chain, chain[0])

                    def rstd(dst, src, scale, n, signal):
                        link(pool.tensor_scalar(dst, src, scale, EPS, ALU.mult, ALU.add))
                        pool.tensor_tensor(dst, dst, neg_half[:, 0:n], ALU.pow).then_inc(signal, 1)

                    def norm():
                        pool.wait_ge(x_squared, NT)
                        rstd(rsx, ssx, 1.0 / D, NT, rms_x)

                    def cols():
                        pool.wait_ge(gates_ready, 2)
                        for s in range(STEPS):
                            for half in range(2):
                                d = half ^ KIND_OF[s]
                                pool.tensor_copy(sel[rows_of(half), s], raw[rows_of(half), TILE_OF[s], :, d * H:d * H + H]).then_inc(selected, 1)

                    def a_norm():
                        pool.wait_ge(summed_a, NT)
                        fs, fr = ssa.rearrange("p t g -> p (t g)"), rsa.rearrange("p t g -> p (t g)")
                        link(pool.tensor_scalar(fr, fs, 0.25, EPS, ALU.mult, ALU.add))
                        link(pool.tensor_tensor(fr, fr, neg_half[:, 0:16], ALU.pow))
                        pool.tensor_scalar(rsa[:, :, 0:H], rsa[:, :, 0:H], 0.5 * HD ** -0.5, None, ALU.mult).then_inc(rms_a, 1)
                        pool.tensor_scalar(rsa[:, :, H:8], rsa[:, :, H:8], 0.5, None, ALU.mult).then_inc(rms_a, 1)

                    def rows(s):
                        j = s % 2
                        if s == 0:
                            pool.wait_ge(sums_ready, 1)
                        if s >= 2:
                            pool.wait_ge(*filled(("gc", s - 2)))
                        dg = prob[:, j].rearrange("p g n -> p (g n)")
                        pool.tensor_tensor(heads(dg, H), over(ident, H), along(cc[:, 0, s, 0:H], P), ALU.mult).then_inc(diag_ready, 1)
                        pool.wait_ge(decay_ready, s + 1)
                        if s >= 2:
                            pool.wait_ge(l_ready, s - 1)
                        pool.tensor_tensor(vk[:, j], st[:, j], along(sel[:, s, 2], P), ALU.mult).then_inc(decay_beta, 1)

                    def solve0(s):
                        j, kind = s % 2, KIND_OF[s]
                        pool.wait_ge(l_ready, s + 1)
                        if s >= 2:
                            pool.wait_ge(*filled(("w", s - 2)))
                        link(pool.tensor_tensor(sX[:, j], lw[:, s], over(K(f"level{kind}_0"), H), ALU.mult))
                        pool.tensor_tensor(sX[:, j], over(ident, H), sX[:, j], ALU.subtract).then_inc(x0_ready, 1)
                        pool.wait_ge(*released(("lt", s)))
                        link(pool.tensor_tensor(sXT[:, j], sLT[:, j], over(K(f"level{1 - kind}_0"), H), ALU.mult))
                        pool.tensor_tensor(sXT[:, j], over(ident, H), sXT[:, j], ALU.subtract).then_inc(x0_ready, 1)

                    def t1(s, n):
                        j, kind = s % 2, KIND_OF[s]
                        if n > 1:
                            pool.wait_ge(*filled(("t1", s, n - 1)))
                        elif s >= 2:
                            pool.wait_ge(*filled(("qd", s - 2)))
                        pool.tensor_tensor(sLm[:, j], sLT[:, j], over(K(f"level{1 - kind}_{n}"), H), ALU.mult).then_inc(lm_ready, 1)

                    def uw(s):
                        j, t = s % 2, TILE_OF[s]
                        pool.wait_ge(terms_ready, 3)
                        if s == 0:
                            pool.wait_ge(l_ready, STEPS)
                        if s >= 1:
                            pool.wait_ge(*filled(("w", s - 1)))
                        pool.tensor_tensor(vk[:, 0], heads(tm[:, t, 2 * BW:3 * BW], H), along(hbeta[:, s], P), ALU.mult).then_inc(scaled_uw, 1)
                        pool.tensor_tensor(vk[:, 1], heads(tm[:, t, BW:2 * BW], H), along(bev[:, s], P), ALU.mult).then_inc(scaled_uw, 1)
                        pool.wait_ge(*filled(("t1", s, LEVELS - 1)))
                        pool.tensor_tensor(sLm[:, j], heads(tm[:, t, 0:BW], H), along(ex[:, 0, s, 0:H], P), ALU.mult).then_inc(scaled_uw, 1)
                        if s >= 2:
                            pool.wait_ge(*filled(("kv", s - 2, 1)))
                        pool.tensor_tensor(kd[:, j], heads(tm[:, t, BW:2 * BW], H), along(ex[:, 1, s, 0:H], P), ALU.mult).then_inc(scaled_uw, 1)

                    def scan_o(s):
                        if 0 < s < STEPS - 1:
                            pool.wait_ge(*filled(("o", s)))
                            pool.wait_ge(*released(("kv", s - 1, 1)))
                            for d in range(2):
                                w = 2 + half_of(d, s)
                                pool.tensor_tensor(st[:, d], st[:, d], along(ex[:, w, s, 0:H], P), ALU.mult).then_inc(st_decayed, 1)

                    def sum_rms(b, t):
                        n = sum_no[(b + "_sum", t)]
                        pool.wait_ge(summed_y, n + 1)
                        k = t + (2 if b == "d" else 0)
                        rstd(rso[:, k], sso[:, k], 1.0 / HD, H, rms_y)

                    def c_prep():
                        pool.wait_ge(params_in, 16 * 13)
                        for w in (0, 2):
                            v = [graw[:, w + i].rearrange("p (a s n) -> p a s n", a=2, s=2) for i in range(2)]
                            for i in range(2):
                                last = pool.tensor_copy(v[1][:, :, i], v[0][:, :, 1 - i])
                                link(last)
                        for w in range(4):
                            src = K(("cos", "sin")[w % 2]).rearrange("p (t n) -> p t n", t=NT)
                            pool.tensor_tensor(rope[:, w], src, over(graw[:, w], NT), ALU.mult).then_inc(rope_ready, 1)
                        pool.wait_ge(summed_c, 1)
                        rstd(rsc.rearrange("p t g -> p (t g)"), ssc.rearrange("p t g -> p (t g)"), 1.0 / HD, 12, rms_c)

                    def b_prep():
                        pool.wait_ge(summed_b, NT)
                        rstd(rsb.rearrange("p t g -> p (t g)"), ssb.rearrange("p t g -> p (t g)"), 1.0 / NAD, 32, rms_b)
                        for t in range(NT):
                            pool.wait_ge(scaled_b, t + 1)
                            for k, gain in enumerate((g_nq, g_nk)):
                                v = heads(btm[:, t, k * BW:(k + 1) * BW], NAH)
                                pool.tensor_tensor(v, v, over(gain, NAH), ALU.mult).then_inc(gained_b, 1)

                    def d_prep():
                        pool.wait_ge(*released(("pj", "d", 0)))
                        pool.memset(vaug[:, :, :, HD:HD + 1], 1.0).then_inc(ones_ready, 1)

                    def d_rows(s):
                        j = s % 2
                        if s == 0:
                            pool.wait_ge(*released(("y", "b", 1)))
                        if s >= 2:
                            pool.wait_ge(*filled(("a", s - 2)))
                        dg = prob[:, j].rearrange("p g n -> p (g n)")
                        pool.tensor_tensor(heads(dg, H), over(ident, H), along(av[:, s], P), ALU.mult).then_inc(diag2_ready, 1)

                    def d_m():
                        pool.wait_ge(m_exp, 2)
                        for par in range(2):
                            pool.tensor_copy(decp[rows_of(par)], dec[rows_of(par), :, :, par:H:2]).then_inc(m_terms, 1)

                    def d_step(s):
                        t = TILE_OF[s]
                        if s == 0:
                            pool.wait_ge(m_terms, 3)
                        pool.tensor_tensor(mq[:, s], heads(dtm[:, t, 0:256], H), along(e_out[:, 0, s], MLK), ALU.mult).then_inc(scaled_d, 1)
                        pool.tensor_tensor(wk[:, s], heads(dtm[:, t, 256:512], H), along(e_out[:, 2, s], MLK), ALU.mult).then_inc(scaled_d, 1)

                    def d_scan(s):
                        if 0 < s < STEPS - 1:
                            pool.wait_ge(*filled(("num", s, 1)))
                            pool.wait_ge(*released(("mkv", s - 1, 1)))
                            for d in range(2):
                                pool.tensor_tensor(cst[:, d], cst[:, d], along(decp[:, s, half_of(d, s)], HD + 1), ALU.mult).then_inc(c_decayed, 1)

                    def branch(n, c):
                        i = branch_no[(n, c)]
                        for t in range(NT):
                            if n != BRANCHES[0]:
                                pool.wait_ge(*released(("branch", n, c, t)))
                                m = merged[:, c, t]
                                pool.tensor_tensor(m, m, gact[i % 2][:, t], ALU.add).then_inc(merge_done, 1)

                    run(norm=norm, cols=cols, a_norm=a_norm, rows=rows, solve0=solve0, t1=t1, uw=uw, scan_o=scan_o,
                        a_sum=lambda t: sum_rms("a", t), d_sum=lambda t: sum_rms("d", t), c_prep=c_prep, b_prep=b_prep,
                        d_prep=d_prep, d_rows=d_rows, d_m=d_m, d_step=d_step, d_scan=d_scan, branch=branch)

            nums = [s.num for s in layer_sems]
            nc.all_engine_barrier()
            nc.sync.sem_clear(range(min(nums), max(nums) + 1))
            nc.all_engine_barrier()

        with nc.Block() as block:
            @block.sync
            def _(sp):
                for t in range(NT):
                    for half in range(2):
                        c = CHUNKS[t][half]
                        sp.dma_start(out[0, c * C:c * C + C, :], x[rows_of(half), t, :]).then_inc(stored, 16)
                sp.wait_ge(stored, 64)


_INS = ["x", "norm_g", "w_in", "conv_a", "dn_a_log", "dn_dt_bias", "dn_norm_g", "na_q_norm", "na_k_norm", "na_rpb",
        "ga_q_norm", "ga_k_norm", "ml_i_bias", "ml_f_bias", "ml_norm_g", "w_branch", "w_out"]


def kernel(**inputs):
    import concourse.bacc as _bacc
    from concourse.bass_utils import run_bass_kernel_spmd as _run

    nc = _bacc.Bacc("TRN2", target_bir_lowering=False, num_devices=1)
    arrays = {f"in_{n}": np.ascontiguousarray(inputs[n]) for n in _INS}
    arrays["in_table"] = np.concatenate(list(constants().values()), axis=1)
    args = [nc.dram_tensor(n, a.shape, mybir.dt.from_np(a.dtype), kind="ExternalInput").ap() for n, a in arrays.items()]
    args.append(nc.dram_tensor("out_x", (1, S, D), F32, kind="ExternalOutput").ap())
    build(nc, *args)
    r = _run(nc, [arrays], core_ids=[0])
    return r.results[0]["out_x"]
```

```python
from contextlib import ExitStack

import numpy as np

import concourse.bass as bass
from concourse import mybir

F32 = mybir.dt.float32
F32R = mybir.dt.float32r
ALU = mybir.AluOpType
ACT = mybir.ActivationFunctionType
X = mybir.AxisListType.X

P = 128
D = 1024
S = 256
DEPTH = 2
NT = S // P
KT = D // P
BW = 512
BK = BW // P
EPS = 1e-6
H = 4
HD = 128
C = 64
STEPS = S // C
NAH, NAD = 8, 64
WIN, GRID = 16, 64
RPB_R, RPB_C = 15, 31
MLK = 64
CONV = 5
CB = 12
LEVELS = 6
BIG = 1e30

A_QKV, A_AB, A_Z = 0, 1536, 1552
B_QKV, B_Z = 2064, 3600
C_QKV, C_Z = 4112, 5136
D_QKV, D_IF, D_O, D_Z = 5648, 6672, 6688, 7200
GATES = 7712
PW = 11808
WB = 256
UK, UN = 2, 4
RAW, PARTS = 4, 4

TILE_OF = (0, 1, 1, 0)
KIND_OF = (0, 0, 1, 1)
CHUNKS = ((0, 3), (1, 2))
BRANCHES = (0, 2, 1, 3)


def half_of(direction, s):
    return direction ^ KIND_OF[s]


def constants():
    i = np.arange(P)
    same = (i[:, None] // C) == (i[None, :] // C)
    lo = (i[:, None] < C) & same
    hi = (i[:, None] >= C) & same
    le, ge = i[:, None] <= i[None, :], i[:, None] >= i[None, :]
    before = [(lo & le) | (hi & ge), (lo & ge) | (hi & le)]
    eye = np.eye(P, dtype=bool)
    out = {"ident": eye, "ones": np.ones((P, P))}
    for k in range(2):
        out[f"cum{k}"] = before[k]
        out[f"after{k}"] = before[1 - k] & ~eye
        out[f"mask{k}"] = np.where(before[1 - k], 0.0, -BIG)
    out["half0"] = np.repeat(i[:, None] < C, P, axis=1)
    out["half1"] = np.repeat(i[:, None] >= C, P, axis=1)
    for k in range(2):
        for n in range(LEVELS):
            b = (i % C) >> n
            down = (b[:, None] % 2 == 1) & (b[None, :] == b[:, None] - 1)
            level = (lo & down) | (hi & down.T) if k == 0 else (lo & down.T) | (hi & down)
            out[f"level{k}_{n}"] = level[:, 0:C] | level[:, C:P]
    tokens = np.stack([np.concatenate([np.arange(C) + C * c for c in CHUNKS[t]]) for t in range(NT)])
    m = HD // 4
    inv = (np.float32(10000.0) ** (-np.arange(m, dtype=np.float32) / np.float32(m))).astype(np.float32)
    row = (tokens // GRID).astype(np.float32)[..., None] * inv
    col = (tokens % GRID).astype(np.float32)[..., None] * inv
    cos = np.concatenate([np.cos(row), np.cos(row), np.cos(col), np.cos(col)], -1)
    sin = np.concatenate([-np.sin(row), np.sin(row), -np.sin(col), np.sin(col)], -1)
    out["cos"] = cos.transpose(1, 0, 2).reshape(P, NT * HD)
    out["sin"] = sin.transpose(1, 0, 2).reshape(P, NT * HD)
    c = np.arange(GRID)
    c0 = np.clip(c - WIN // 2, 0, GRID - WIN)
    win = (c[None, :] >= c0[:, None]) & (c[None, :] < c0[:, None] + WIN)
    out["window"] = np.tile(np.where(win, 0.0, -BIG), (2, 1))
    z = (np.arange(P)[:, None] + np.arange(P)[None, :] == 78) & (np.arange(P)[:, None] < RPB_C)
    out["toeplitz"] = z
    pick = np.zeros((P, NAH * 7))
    for h in range(NAH):
        for o in range(7):
            pick[h * RPB_R + 4 + o, h * 7 + o] = 1
    out["pick"] = pick
    return {k: np.asarray(v, np.float32) for k, v in out.items()}


def const_layout():
    at, where = 0, {}
    for name, a in constants().items():
        where[name] = (at, a.shape[1])
        at += a.shape[1]
    return where, at


def order():
    def proj(kind, n):
        return [("proj", kind, i) for i in range(n)]

    def gates(n):
        return [g for c in range(2) for g in (("proj", "gate", (n, c, 0)), ("proj", "gate", (n, c, 1)), ("branch", n, c))]

    streamed = iter(proj("za", 2) + proj("c", 4) + proj("zc", 2) + proj("b", 6) + proj("zb", 2) + proj("d", 4)
                    + proj("o", 2) + proj("zd", 2) + [g for n in BRANCHES for g in gates(n)])
    o = []

    def stream():
        step = next(streamed, None)
        if step and step[:2] == ("proj", "gate") and step[2][1:] == (0, 1):
            o.append(("y_parts", step[2][0]))
        if step:
            o.append(step)
        return step

    def add(*steps):
        for step in steps:
            if isinstance(step, int):
                for _ in range(step):
                    stream()
            else:
                o.append(step)

    add(("norm",), ("rope",), ("proj", "conv", 0), ("conv", 0), ("proj", "conv", 1), ("conv", 1), ("silu", 0), ("gatecols",),
        ("proj", "conv", 2), ("conv", 2), ("silu", 1), ("gatecols_turn",), ("proj", "conv", 3), ("conv", 3), ("silu", 2), 1, ("a_turn", 0),
        ("silu", 3), ("proj", "conv", 4), ("cols",), ("conv", 4), ("a_turn", 1), ("a_norm",), ("proj", "conv", 5), ("silu", 4), ("a_scale",), ("conv", 5),
        1, ("silu", 5), ("a_qkt",), 1, ("a_kkqk",), ("a_turn", 2), 1)

    def solve(s):
        a = [("solve0", s), ("solve0", s + 1)]
        for n in range(1, LEVELS):
            a += [("t1", s, n), ("t1", s + 1, n), ("update", s, n), ("update", s + 1, n)]
        return a

    groups = [(t, q) for t in range(NT) for q in range(2)]
    attention = [("c_qkt",)]
    for n, g in enumerate(groups):
        attention += [("c_score", *g)] + ([("c_mix", *groups[n - 1])] if n else []) + [("c_turn", *g)]
    attention += [("c_mix", *groups[-1]), ("c_sum", 0), ("c_sum", 1), ("c_out", 0), ("c_out", 1)]

    def weave(*parts):
        keyed = [(a + (k + 0.5) / len(steps) * (b - a), j, step) for j, (steps, a, b) in enumerate(parts) for k, step in enumerate(steps)]
        return [step for _, _, step in sorted(keyed, key=lambda v: v[:2])]

    first = weave((solve(0), 0, 1), ([("c_prep",), ("c_rotate", 0), ("c_rotate", 1)], 0, 0.15), (attention, 0.25, 1),
                  ([("rows", 2), ("rows", 3)], 0.1, 0.95), ([1] * 8, 0, 1))
    second = weave((solve(2), 0, 1), ([("scan_v", 1), ("scan_o", 1)], 0, 1), ([("b_square",), ("b_prep",)], 0.05, 0.75), ([1] * 6, 0.2, 0.9))
    add(("rows", 0), 1, ("rows", 1), 1, *first, ("uw", 0), 1, ("uw", 1), ("scan_v", 0), ("scan_o", 0), *second)
    add(("uw", 2), ("scan_v", 2), ("uw", 3), ("b_bias", 0), ("b_bias", 1), ("scan_o", 2), 1, ("b_bias", 2), ("scan_v", 3), ("b_bias", 3),
        ("scan_o", 3), ("a_sum",), ("b_bias", 4), 1, ("a_gate", 0), ("a_gate", 1), ("b_bias", 5), 1, ("a_out", 0), ("a_out", 1), 2,
        ("b_bias", 6), ("b_bias", 7))
    add(("b_turn_in",), ("d_rows", 0), ("d_rows", 1), 1, ("d_rows", 2), ("d_rows", 3), 1, ("d_prep",), ("b_score", *groups[0]), ("b_score", *groups[1]))
    for n, g in enumerate(groups):
        add(("b_turn", *g), 1, ("b_mix", *g))
        if n + 2 < len(groups):
            add(("b_score", *groups[n + 2]))
        if n == 1:
            add(("d_m",))
    add(("b_sum", 0), ("b_sum", 1), 2, ("b_out", 0), ("b_out", 1))
    add(("d_step", 0), ("d_step", 1), ("d_turn", 0), 1, ("d_step", 2), ("d_turn", 1), 1, ("d_step", 3), ("d_turn", 2), 1, ("d_turn", 3))
    add(("d_scan", 0), 1, ("d_scan", 1), 1, ("d_scan", 2), 1, ("d_scan", 3), ("d_den",), ("d_sum",), 1, ("d_gate", 0), ("d_gate", 1), 1, ("d_out", 0), ("d_out", 1))
    while stream():
        pass
    return o[:-1] + [("merge_turn", 0), ("merged", 0), o[-1], ("merged", 1)] + proj("out", 4)


def weight_plan(stages):
    first = {"conv": A_QKV, "za": A_Z, "c": C_QKV, "zc": C_Z, "b": B_QKV, "zb": B_Z, "d": D_QKV, "o": D_O, "zd": D_Z, "out": 0}
    plan = []
    for name, *args in stages:
        if name == "branch":
            plan.append(("branch", tuple(args), args[1] * 512))
        elif name == "proj" and args[0] == "gate":
            n, c, i = args[1]
            plan.append(("gate", args[1], GATES + n * D + c * 512 + WB * i))
        elif name == "proj":
            plan.append((args[0], args[1], first[args[0]] + WB * args[1]))
    return plan


def build(nc, x_in, norm_g, w_in, conv_a, dn_a_log, dn_dt_bias, dn_norm_g, na_q_norm, na_k_norm, na_rpb,
          ga_q_norm, ga_k_norm, ml_i_bias, ml_f_bias, ml_norm_g, w_branch, w_out, table, out):
    ctx = ExitStack()
    with ctx:
        def sb(name, *free):
            return ctx.enter_context(nc.sbuf_tensor(name, [P, *free], F32))

        class Region:

            def __init__(self, t, at, size):
                self.t, self.at, self.size = t, at, size

            def cut(self, **dims):
                n = int(np.prod(list(dims.values())))
                assert self.at + n <= self.size, (self.at + n, self.size)
                v = self.t[:, self.at:self.at + n]
                self.at += n
                names = " ".join(dims)
                return v if len(dims) == 1 else v.rearrange(f"p ({names}) -> p {names}", **dims)

        where, n_const = const_layout()
        tab = sb("tab", n_const)

        def K(name):
            a, n = where[name]
            return tab[:, a:a + n]

        def over(v, n):
            return v[:, None, :].to_broadcast([v.shape[0], n, v.shape[1]])

        def along(v, n):
            return v[:, :, None].to_broadcast([v.shape[0], v.shape[1], n])

        h_high, h_low = sb("h_high", KT, S)[:], sb("h_low", KT, S)[:]
        y_high, y_low = sb("y_high", BK, S)[:], sb("y_low", BK, S)[:]
        w_high, w_low = sb("w_high", PARTS, UK, WB), sb("w_low", PARTS, UK, WB)
        ring = sb("ring", RAW, UK, WB)
        zbuf = sb("zbuf", 4, NT, BW)
        z = [zbuf[:, k] for k in (0, 2, 1, 3)]
        merged = zbuf[:, 0:2]
        yT = [None, None, sb("yT2", BK, S)[:], None]
        n_small = 2000
        small = Region(sb("small", n_small), 0, n_small)
        colp = small.cut(a=CONV * CB + KT)
        g_dn, g_ml = small.cut(a=HD), small.cut(a=HD)
        g_nq, g_nk = small.cut(a=NAD), small.cut(a=NAD)
        g_gate = small.cut(k=4, e=8)
        neg_half = small.cut(a=32)
        ssx, rsx = small.cut(a=NT), small.cut(a=NT)
        gps = small.cut(t=NT, e=32)
        raw = small.cut(t=NT, k=4, e=8)
        softp = small.cut(t=NT, k=2, e=8)
        coef = small.cut(k=2, e=8)
        sel = small.cut(s=STEPS, k=4, h=H)
        cc = small.cut(w=4, s=STEPS, e=8)
        ex = small.cut(w=4, s=STEPS, e=8)
        av = small.cut(s=STEPS, h=H)
        bev = small.cut(s=STEPS, h=H)
        hbeta = small.cut(s=STEPS, h=H)
        amx = small.cut(s=STEPS, h=H, k=2)
        cm = small.cut(s=STEPS, h=H)
        mst = small.cut(s=STEPS, k=2, h=H)
        mxs = small.cut(s=STEPS, k=2, h=H)
        msel, mxsel = small.cut(s=STEPS, h=H), small.cut(s=STEPS, h=H)
        mrun = small.cut(s=STEPS, h=H)
        e_in, e_out = small.cut(k=3, s=STEPS, h=H), small.cut(k=3, s=STEPS, h=H)
        dec_in, dec = small.cut(s=STEPS, k=2, h=H), small.cut(s=STEPS, k=2, h=H)
        decp = small.cut(s=STEPS, k=2, u=2)
        ssa, rsa = small.cut(t=NT, g=8), small.cut(t=NT, g=8)
        ssb, rsb = small.cut(t=NT, g=16), small.cut(t=NT, g=16)
        ssc, rsc = small.cut(t=NT, g=6), small.cut(t=NT, g=6)
        nmc, smc, rmc = small.cut(t=NT, h=H), small.cut(t=NT, h=H), small.cut(t=NT, h=H)
        nmb, smb, rmb = small.cut(t=NT, h=NAH), small.cut(t=NT, h=NAH), small.cut(t=NT, h=NAH)
        sso, rso = small.cut(b=4, h=H), small.cut(b=4, h=H)
        rpbT = small.cut(a=NAH * 7)
        den, nden = small.cut(s=STEPS, h=H), small.cut(s=STEPS, h=H)

        n_big = 19504
        big = sb("big", n_big)
        r = Region(big, 0, n_big)
        cin = r.cut(b=CB, n=S + CONV - 1)
        cac = r.cut(b=CB, n=S)
        q = Region(big, 0, r.at)
        sX, sXT = q.cut(j=2, h=H, n=P), q.cut(j=2, h=H, n=P)
        sLT, sT1 = q.cut(j=2, h=H, n=P), q.cut(j=2, h=H, n=P)
        sLm = q.cut(j=2, h=H, n=P)
        vn = q.cut(h=H, n=P)
        vk = r.cut(w=2, h=H, n=P)
        tm = r.cut(t=NT, n=3 * BW)
        h_raw = tm.rearrange("p t n -> p (t n)")[:, 0:KT * S].rearrange("p (k n) -> p k n", k=KT)
        qkt = r.cut(g=8, n=S)
        us = qkt.rearrange("p (s g) n -> p s (g n)", s=STEPS).rearrange("p s (h n) -> p s h n", h=H)
        kkqk = r.cut(t=NT, w=2, h=H, n=P)
        qdT, kd = kkqk[:, 0], kkqk[:, 1]
        taps = kkqk.rearrange("p t w h n -> p (t w h n)")[:, 0:CONV * S].rearrange("p (j n) -> p j n", j=CONV)
        lw = r.cut(s=STEPS, h=H, n=P)
        qkd = r.cut(s=STEPS, h=H, n=P)
        csl = big[:, r.at - 4096:r.at - 1024].rearrange("p (b n) -> p b n", b=CB)
        st = r.cut(d=2, h=H, n=P)
        r = Region(big, 0, n_big)
        bias = r.cut(t=NT, h=NAH, n=S)
        nqT, nkT = r.cut(g=4, n=S), r.cut(g=4, n=S)
        yT[1], yT[3] = r.cut(g=BK, n=S), r.cut(g=BK, n=S)
        mqk_T = r.cut(t=NT, g=4, n=P)
        mqk = r.cut(t=NT, h=H, n=P)
        mS = r.cut(s=STEPS, h=H, n=P)
        mqT = r.cut(s=STEPS, g=2, n=P)
        mq = r.cut(s=STEPS, h=H, n=MLK)
        wk = r.cut(s=STEPS, h=H, n=MLK)
        cst = r.cut(d=2, g=2, n=HD + 1)
        num = r.cut(s=STEPS, h=H, n=HD + 1)
        yT[0] = r.cut(g=BK, n=S)
        n_mid = 8192
        mid = sb("mid", n_mid)
        r = Region(mid, 0, n_mid)
        ctm = r.cut(t=NT, n=1024)
        xh = ctm
        crp = r.cut(t=NT, n=768)
        cqT = r.cut(g=6, n=S)
        rope = r.cut(w=4, t=NT, n=HD)
        graw = r.cut(w=4, n=HD)
        prob = r.cut(j=2, g=2, n=S)
        probT = r.cut(g=2, k=2, n=P)
        r = Region(mid, r.at - 512, n_mid)
        w_small = r.cut(k=KT, n=32)
        small_parts = [v.rearrange("p g n -> p (g n)")[:, 0:KT * 32 + 96] for v in (y_high, y_low)]
        small_T = prob.rearrange("p j g n -> p (j g n)")[:, 0:S]
        rawp = r.cut(a=P)
        rpb = r.cut(a=RPB_C)
        btm = sb("btm", NT, 3 * BW)
        x = btm[:, :, 0:D]
        r = Region(mid, 0, n_mid)
        dtm = r.cut(t=NT, n=512)
        vaug = r.cut(t=NT, h=H, n=HD + 1)
        gact0 = r.cut(t=NT, n=512)
        og = rope.rearrange("p w t n -> p (w t n)").rearrange("p (t n) -> p t n", t=NT)
        assert r.at <= 2048 + 1536
        gact = [gact0, cqT.rearrange("p g n -> p (g n)")[:, 0:1024].rearrange("p (t n) -> p t n", t=NT)]

        ident_in = ctx.enter_context(nc.semaphore("ident_in"))
        table_in = ctx.enter_context(nc.semaphore("table_in"))
        x_loaded = ctx.enter_context(nc.semaphore("x_loaded"))
        stored = ctx.enter_context(nc.semaphore("stored"))
        setup_done = ctx.enter_context(nc.semaphore("setup_done"))

        layer_sems = []

        def sem(name):
            s = ctx.enter_context(nc.semaphore(name))
            layer_sems.append(s)
            return s

        class Bank:

            def __init__(self, name):
                self.t = ctx.enter_context(nc.psum_tensor(name, [P, 512], F32))[:, :]
                self.full, self.free, self.fills = sem(name + "_full"), sem(name + "_free"), 0
                self.signals = 0

        pj = [Bank("pj0"), Bank("pj1")]
        mb = [Bank(f"mb{i}") for i in range(6)]
        filling = {}

        def room(bank, key):
            assert key not in filling
            bank.fills += 1
            if key[0] not in ("pj", "branch"):
                bank.signals += 1
            filling[key] = (bank, bank.fills, bank.signals)
            return bank.free, bank.fills - 1

        def filled(key):
            bank, _, n = filling[key]
            return bank.full, n

        def released(key):
            bank, n, _ = filling[key]
            return bank.free, n

        def bank_of(key):
            return filling[key][0]

        ring_full = [sem(f"ring_full{i}") for i in range(RAW)]
        w_rounded = sem("w_rounded")
        w_split = sem("w_split")
        weights_used = sem("weights_used")
        small_rounded = sem("small_rounded")
        small_split = sem("small_split")
        h_rounded = sem("h_rounded")
        h_split = sem("h_split")
        y_rounded = sem("y_rounded")
        y_split = sem("y_split")
        m_rounded = sem("m_rounded")
        x_saved = sem("x_saved")
        x_back = sem("x_back")
        colp_in = sem("colp_in")
        cols_in = sem("cols_in")
        params_in = sem("params_in")
        dve_chain = sem("dve_chain")
        pool_chain = sem("pool_chain")
        padded = sem("padded")
        x_squared = sem("x_squared")
        rms_x = sem("rms_x")
        h_ready = sem("h_ready")
        taps_ready = sem("taps_ready")
        conv_out = sem("conv_out")
        conv_out_odd = sem("conv_out_odd")
        conv_act = sem("conv_act")
        silu_ready = sem("silu_ready")
        z_tanh = sem("z_tanh")
        softplus_in = sem("softplus_in")
        gate_exp = sem("gate_exp")
        gates_ready = sem("gates_ready")
        selected = sem("selected")
        sums_ready = sem("sums_ready")
        terms_ready = sem("terms_ready")
        squared_a = sem("squared_a")
        summed_a = sem("summed_a")
        rms_a = sem("rms_a")
        normed_a = sem("normed_a")
        diag_ready = sem("diag_ready")
        decay_arg = sem("decay_arg")
        decay_ready = sem("decay_ready")
        decay_beta = sem("decay_beta")
        l_ready = sem("l_ready")
        x0_ready = sem("x0_ready")
        xt0_ready = sem("xt0_ready")
        lm_ready = sem("lm_ready")
        scaled_uw = sem("scaled_uw")
        vn_ready = sem("vn_ready")
        st_decayed = sem("st_decayed")
        rope_ready = sem("rope_ready")
        squared_c = sem("squared_c")
        summed_c = sem("summed_c")
        rms_c = sem("rms_c")
        rotated = sem("rotated")
        c_max = sem("c_max")
        squared_b = sem("squared_b")
        summed_b = sem("summed_b")
        rms_b = sem("rms_b")
        gained_b = sem("gained_b")
        b_max = sem("b_max")
        b_prob = sem("b_prob")
        y_summed = sem("y_summed")
        squared_y = sem("squared_y")
        summed_y = sem("summed_y")
        rms_y = sem("rms_y")
        y_ready = sem("y_ready")
        ones_ready = sem("ones_ready")
        diag2_ready = sem("diag2_ready")
        m_args = sem("m_args")
        m_exp = sem("m_exp")
        m_terms = sem("m_terms")
        s_arg = sem("s_arg")
        s_exp = sem("s_exp")
        s_ready = sem("s_ready")
        scaled_d = sem("scaled_d")
        c_decayed = sem("c_decayed")
        merge_done = sem("merge_done")

        stages = order()
        plan = weight_plan(stages)
        block_no = {(k, a): n for n, (k, a, _) in enumerate(plan)}
        def r32(v):
            return v.bitcast(F32R)

        def products_done(kind, arg):
            return weights_used, UN * (block_no[(kind, arg)] + 1)
        ident, ones = K("ident"), K("ones")
        PARAMS = 11

        def halves(v):
            return v.rearrange("p h (k n) -> p (h k) n", k=2)

        def rows_of(half):
            return slice(half * C, half * C + C)

        def heads(v, n):
            return v.rearrange("p (h n) -> p h n", h=n)

        def solve_no(s, n):
            return (s // 2) * 2 * (LEVELS - 1) + (n - 1) * 2 + s % 2

        def group_no(t, k):
            return t * 2 + k

        y_order = [a for a in stages if a[0] in ("a_out", "b_out", "c_out", "d_out")]
        y_no = {a: n for n, a in enumerate(y_order)}
        sum_order = [a for a in stages if a[0] in ("a_sum", "d_sum")]
        sum_no = {a[0][0]: NT * n for n, a in enumerate(sum_order)}
        z_order = [a[1:] for a in stages if a[0] == "proj" and a[1] in ("za", "zb", "zc", "zd")]
        z_no = {a: n for n, a in enumerate(z_order)}
        branch_list = [a[1:] for a in stages if a[0] == "branch"]
        branch_no = {(n, c): i for i, (n, c) in enumerate(a[1:] for a in stages if a[0] == "branch")}
        o_sum = {"a": [us[:, 0], us[:, 1]], "d": [mqk[:, 0], mqk[:, 1]]}
        o_sq = {"a": [us[:, 3], us[:, 2]], "d": [mqk_T[:, 0], mqk_T[:, 1]]}
        y_tile = {"a": [v.rearrange("p h n -> p (h n)") for v in o_sum["a"]],
                  "d": [v.rearrange("p h n -> p (h n)") for v in o_sum["d"]],
                  "b": [btm[:, t, 0:BW] for t in range(NT)], "c": [crp[:, t, 0:BW] for t in range(NT)]}
        probTs = [probT, mq.rearrange("p s h n -> p (s h n)")[:, 0:512].rearrange("p (g k n) -> p g k n", g=2, k=2)]
        b_probs = [prob, wk.rearrange("p s h n -> p (s h n)").rearrange("p (j g n) -> p j g n", j=2, g=2)]
        diag = [heads(prob[:, j].rearrange("p g n -> p (g n)"), H) for j in range(2)] + [us[:, 2], us[:, 3]]
        product_banks, turn = {}, 0
        for a in stages:
            if a[0] == "branch" or a[:2] in (("proj", "gate"), ("proj", "out")):
                n = NT if a[0] == "branch" else 1
                product_banks[a] = [(pj + mb[5:])[(turn + t) % 3] for t in range(n)]
                turn += n
            elif a[0] == "proj":
                product_banks[a] = [pj[turn % 2]]
                turn += 1

        def run(split=None, **steps):
            for name, *args in stages:
                if split and name in ("proj", "branch"):
                    n = block_no[(args[0], args[1])] if name == "proj" else block_no[("branch", tuple(args))]
                    for u in range(UN * n + PARTS, min(UN * (n + 1) + PARTS, UN * len(plan))):
                        split(u)
                if name in steps:
                    steps[name](*args)

        with nc.Block() as block:
            @block.sync
            def _(sp):
                for t in range(NT):
                    for half in range(2):
                        c = CHUNKS[t][half]
                        sp.dma_start(x[rows_of(half), t, :], x_in[0, c * C:c * C + C, :]).then_inc(x_loaded, 16)
                sp.dma_start(tab[:, P:n_const], table[:, P:n_const]).then_inc(table_in, 16)
                sp.wait_ge(ident_in, 16)
                sp.wait_ge(x_loaded, 64)

            @block.scalar
            def _(act):
                act.dma_start(tab[:, 0:P], table[:, 0:P]).then_inc(ident_in, 16)

            @block.vector
            def _(dve):
                nc.vector.memset(neg_half, -0.5).then_inc(setup_done, 1)

        with nc.Fori(0, DEPTH) as layer:
            with nc.Block() as block:
                @block.tensor
                def _(pe):
                    mm, tr = nc.tensor.matmul, nc.tensor.transpose

                    def turn4(bank, parts, width=P):
                        for k, v in enumerate(parts):
                            last = tr(bank.t[0:width, k * P:(k + 1) * P], v, ident)
                        return last.then_inc(bank.full, 1)

                    def split_product(o, lhs, rhs, start, stop):
                        (a, a_low), (b, b_low) = lhs, rhs
                        mm(o, r32(a), r32(b), start=start, stop=False, skip_group_check=True)
                        mm(o, r32(a), r32(b_low), start=False, stop=False, skip_group_check=True)
                        return mm(o, r32(a_low), r32(b), start=False, stop=stop, skip_group_check=True)

                    def norm():
                        pe.wait_ge(colp_in, 32)
                        pe.wait_ge(*room(mb[4], "colp"))
                        n = CONV * CB + KT
                        tr(mb[4].t[:, 0:n], rawp[0:n, :], ident[0:n, 0:n]).then_inc(mb[4].full, 1)
                        for q in range(2):
                            for t in range(NT):
                                pe.wait_ge(h_ready, t + 1)
                                b = mb[2 * t + q]
                                pe.wait_ge(*room(b, ("hT", t, q)))
                                turn4(b, [xh[:, t, (4 * q + k) * P:(4 * q + k + 1) * P] for k in range(4)])

                    def gatecols():
                        pe.wait_ge(table_in, 16)
                        pe.wait_ge(params_in, 16 * PARAMS)
                        pe.wait_ge(*room(mb[5], "rpb"))
                        m = NAH * RPB_R
                        mm(mb[5].t[0:RPB_C, 0:NAH * 7], rpb[0:m, :], K("pick")[0:m, :], start=True, stop=True).then_inc(mb[5].full, 1)
                        pe.wait_ge(small_split, 3)
                        pe.wait_ge(*room(mb[4], "small"))
                        for k in range(KT):
                            w = [v[:, k * 32:k * 32 + P] for v in small_parts]
                            last = split_product(mb[4].t[:, 0:S], w, (h_high[:, k], h_low[:, k]), k == 0, k == KT - 1)
                        last.then_inc(mb[4].full, 1)

                    def gatecols_turn():
                        pe.wait_ge(*released("small"))
                        pe.wait_ge(*room(mb[5], "gatecols"))
                        for t in range(NT):
                            last = tr(mb[5].t[:, t * 32:(t + 1) * 32], small_T[0:32, t * P:(t + 1) * P], ident[0:32, 0:32])
                        last.then_inc(mb[5].full, 1)

                    def proj(kind, arg):
                        n = block_no[(kind, arg)]
                        b = product_banks[("proj", kind, arg)][0]
                        if kind == "out" and arg == 0:
                            pe.wait_ge(*released(("mT", 1, 0)))
                        pe.wait_ge(*room(b, ("pj", kind, arg)))
                        for u in range(UN):
                            unit = UN * n + u
                            if kind == "out" and arg == 0 and u == UN // 2:
                                merged_turn(1)
                                pe.wait_ge(*released(("mT", 1, 1)))
                            if kind == "conv" and arg == 0:
                                pe.wait_ge(h_split, 2 * (u * UK // 4) + 2)
                            pe.wait_ge(w_split, unit + 1)
                            for i in range(2):
                                o = b.t[:, i * WB:(i + 1) * WB]
                                for k in range(UK):
                                    w = [v[:, unit % PARTS, k] for v in (w_high, w_low)]
                                    h = [v[:, u * UK + k] for v in (h_high, h_low)]
                                    flags = dict(start=(u == 0 and i == 0 and k == 0), stop=(u == UN - 1 and k == UK - 1))
                                    sl = slice(i * P, (i + 1) * P)
                                    if kind == "conv":
                                        last = split_product(o, [v[:, sl] for v in w], h, **flags)
                                    else:
                                        last = split_product(o, [v[:, sl] for v in h], w, **flags)
                            last.then_inc(weights_used, 1)

                    def a_turn(q):
                        pe.wait_ge(silu_ready, 8 * (q + 1))
                        for t in range(NT):
                            b = mb[(2 * q + t) % 4]
                            pe.wait_ge(*room(b, ("tm", t, q)))
                            turn4(b, [csl[:, 4 * q + k, t * P:(t + 1) * P] for k in range(4)])

                    def a_qkt():
                        for t in range(NT):
                            pe.wait_ge(normed_a, t + 1)
                            for q in range(2):
                                b = mb[2 * t + q]
                                pe.wait_ge(*room(b, ("qkt", t, q)))
                                turn4(b, [tm[:, t, (4 * q + k) * P:(4 * q + k + 1) * P] for k in range(4)])

                    def a_kkqk():
                        for t in range(NT):
                            pe.wait_ge(*released(("qkt", t, 1)))
                            sl = slice(t * P, t * P + P)
                            for w in range(2):
                                b = mb[2 * t + w]
                                pe.wait_ge(*room(b, ("kkqk", t, w)))
                                for h in range(H):
                                    lhs = qkt[:, (H if w == 0 else 0) + h, sl]
                                    last = mm(b.t[:, h * P:(h + 1) * P], lhs, qkt[:, H + h, sl], start=True, stop=True)
                                last.then_inc(b.full, 1)

                    def cols():
                        pe.wait_ge(selected, 8)
                        pe.wait_ge(*room(mb[5], "cols"))
                        def gl(a, b):
                            return sel[:, a:b, 0:2, :].rearrange("p s k h -> p s (k h)")
                        o = mb[5].t[:, 0:P].rearrange("p (w s e) -> p w s e", w=4, s=STEPS)
                        for kind in range(2):
                            s0 = 2 * kind
                            mm(o[:, 0, s0:s0 + 2], K(f"cum{kind}"), gl(s0, s0 + 2), start=True, stop=True)
                            mm(o[:, 1, s0:s0 + 2], K(f"after{kind}"), gl(s0, s0 + 2), start=True, stop=True)
                        for half in range(2):
                            last = mm(o[:, 2 + half], K(f"half{half}"), gl(0, STEPS), start=True, stop=True)
                        last.then_inc(mb[5].full, 1)

                    def rows(s):
                        j = s % 2
                        pe.wait_ge(diag_ready, s + 1)
                        pe.wait_ge(*room(mb[j], ("gc", s)))
                        mm(mb[j].t[:, :], ones, diag[s].rearrange("p h n -> p (h n)"), start=True, stop=True).then_inc(mb[j].full, 1)

                    def solve0(s):
                        j = s % 2
                        pe.wait_ge(l_ready, s + 1)
                        pe.wait_ge(*room(mb[j], ("lt", s)))
                        turn4(mb[j], [lw[:, s, h] for h in range(H)])
                        pe.wait_ge(*room(mb[2 + j], ("qkdt", s)))
                        turn4(mb[2 + j], [qkd[:, s, h] for h in range(H)])

                    def product(bank, lhs, rhs):
                        for h in range(H):
                            last = mm(bank.t[:, h * P:(h + 1) * P], lhs[:, h], rhs[:, h], start=True, stop=True)
                        last.then_inc(bank.full, 1)

                    def t1(s, n):
                        j = s % 2
                        pe.wait_ge(lm_ready, solve_no(s, n) + 1)
                        if n == 1:
                            pe.wait_ge(x0_ready, s + 1)
                        else:
                            pe.wait_ge(*released(("dxt", s, n - 1)))
                        pe.wait_ge(*room(mb[j], ("t1", s, n)))
                        product(mb[j], sLm[:, j], sX[:, j])

                    def update(s, n):
                        j = s % 2
                        pe.wait_ge(*released(("t1", s, n)))
                        if n == 1:
                            pe.wait_ge(xt0_ready, s + 1)
                        if n < LEVELS - 1:
                            pe.wait_ge(*room(mb[2 + j], ("dx", s, n)))
                            product(mb[2 + j], sXT[:, j], sT1[:, j])
                        pe.wait_ge(*room(mb[j], ("dxt", s, n)))
                        product(mb[j], sT1[:, j], sXT[:, j])

                    def uw(s):
                        j = s % 2
                        pe.wait_ge(*released(("dxt", s, LEVELS - 1)))
                        pe.wait_ge(scaled_uw, 4 * s + 2)
                        pe.wait_ge(*room(mb[j], ("u", s)))
                        product(mb[j], sXT[:, j], vk[:, 0])
                        pe.wait_ge(*room(mb[2 + j], ("w", s)))
                        product(mb[2 + j], vk[:, 1], sXT[:, j])
                        pe.wait_ge(scaled_uw, 4 * s + 3)
                        pe.wait_ge(*room(mb[j], ("qd", s)))
                        turn4(mb[j], [sLm[:, j, h] for h in range(H)])

                    def scan_v(s):
                        if s == 0:
                            return
                        pe.wait_ge(*released(("w", s)))
                        pe.wait_ge(*released(("kv", s - 1, 1)))
                        pe.wait_ge(*room(mb[4], ("ws", s)))
                        for h in range(H):
                            for half in range(2):
                                last = mm(mb[4].t[rows_of(half), h * P:(h + 1) * P], lw[:, s, h, rows_of(half)],
                                          st[:, half ^ KIND_OF[s], h], start=True, stop=True)
                        last.then_inc(mb[4].full, 1)

                    def scan_o(s):
                        j = s % 2
                        pe.wait_ge(*released(("qd", s)))
                        pe.wait_ge(*released(("qkdt", s)))
                        pe.wait_ge(*(released(("ws", s)) if s else (vn_ready, 1)))
                        pe.wait_ge(*room(mb[5], ("o", s)))
                        for h in range(H):
                            o = mb[5].t[:, h * P:(h + 1) * P]
                            if s > 0:
                                for half in range(2):
                                    mm(o[rows_of(half)], qdT[:, j, h, rows_of(half)], st[:, half ^ KIND_OF[s], h],
                                       start=True, stop=False, skip_group_check=True)
                            last = mm(o, qkd[:, s, h], vn[:, h], start=(s == 0), stop=True, skip_group_check=True)
                        last.then_inc(mb[5].full, 1)
                        if s == STEPS - 1:
                            return
                        pe.wait_ge(scaled_uw, 4 * s + 4)
                        for d in range(2):
                            b, r = mb[4 + d], rows_of(half_of(d, s))
                            pe.wait_ge(*room(b, ("kv", s, d)))
                            for h in range(H):
                                last = mm(b.t[:, h * P:(h + 1) * P], kd[r, j, h], vn[r, h], start=True, stop=True)
                            last.then_inc(b.full, 1)

                    def y_turn(name, t, bank, n):
                        pe.wait_ge(y_ready, y_no[(name + "_out", t)] + 1)
                        pe.wait_ge(*room(bank, ("y", name, t)))
                        turn4(bank, [y_tile[name][t][:, k * P:(k + 1) * P] for k in range(BK)])

                    def c_qkt():
                        for t in range(NT):
                            pe.wait_ge(rotated, t + 1)
                            pe.wait_ge(*room(mb[4], ("cq", t)))
                            turn4(mb[4], [crp[:, t, k * P:(k + 1) * P] for k in range(4)])
                            pe.wait_ge(*room(mb[5], ("ck", t)))
                            turn4(mb[5], [crp[:, t, k * P:(k + 1) * P] for k in range(4, 6)])

                    def c_score(t, q):
                        pe.wait_ge(*released(("ck", 1)))
                        pe.wait_ge(*room(mb[4], ("cs", t, q)))
                        for m in range(2):
                            last = mm(mb[4].t[:, m * S:(m + 1) * S], cqT[:, 2 * q + m, t * P:(t + 1) * P], cqT[:, 4 + q, :], start=True, stop=True)
                        last.then_inc(mb[4].full, 1)

                    def c_turn(t, q):
                        pe.wait_ge(*released(("cs", t, q)))
                        pe.wait_ge(*room(mb[5], ("cp", t, q)))
                        turn4(mb[5], [prob[:, q, m, k * P:(k + 1) * P] for m in range(2) for k in range(NT)])

                    def c_mix(t, q):
                        pe.wait_ge(*released(("cp", t, q)))
                        pe.wait_ge(*room(mb[4], ("co", t, q)))
                        for m in range(2):
                            for k in range(NT):
                                last = mm(mb[4].t[:, m * P:(m + 1) * P], probT[:, m, k], ctm[:, k, 768 + q * HD:768 + (q + 1) * HD],
                                          start=(k == 0), stop=(k == NT - 1))
                        last.then_inc(mb[4].full, 1)

                    def b_bias(i):
                        b = mb[i % 2]
                        pe.wait_ge(*released("rpb"))
                        pe.wait_ge(*room(b, ("bias", i)))
                        z1 = K("toeplitz")[0:RPB_C]
                        for k in range(8):
                            c = 8 * i + k
                            last = mm(b.t[0:C, k * 56:(k + 1) * 56], z1[:, GRID - 1 - c:2 * GRID - 1 - c], rpbT[0:RPB_C, :], start=True, stop=True)
                        last.then_inc(b.full, 1)

                    def b_turn_in():
                        for t in range(NT):
                            pe.wait_ge(gained_b, t + 1)
                            for w in range(2):
                                pe.wait_ge(*room(mb[2 + w], ("nqk", t, w)))
                                turn4(mb[2 + w], [btm[:, t, w * BW + k * P:w * BW + (k + 1) * P] for k in range(4)])

                    def b_score(t, q):
                        pe.wait_ge(*released(("nqk", 1, 1)))
                        for par in range(2):
                            b, r = mb[par], rows_of(par)
                            pe.wait_ge(*room(b, ("bs", t, q, par)))
                            for m in range(2):
                                last = mm(b.t[:, m * S:(m + 1) * S], nqT[r, 2 * q + m, t * P:(t + 1) * P], nkT[r, 2 * q + m, :], start=True, stop=True)
                            last.then_inc(b.full, 1)

                    def b_turn(t, q):
                        for par in range(2):
                            pe.wait_ge(b_prob, 2 * group_no(t, q) + par + 1)
                            pe.wait_ge(*room(mb[2 + par], ("bp", t, q, par)))
                            turn4(mb[2 + par], [b_probs[q][:, par, m, k * P:(k + 1) * P] for m in range(2) for k in range(NT)])

                    def b_mix(t, q):
                        pe.wait_ge(*room(mb[4], ("bo", t, q)))
                        for par in range(2):
                            pe.wait_ge(*released(("bp", t, q, par)))
                            for m in range(2):
                                i, h = 2 * m + par, 4 * q + 2 * m + par
                                for k in range(NT):
                                    last = mm(mb[4].t[:, i * NAD:(i + 1) * NAD], probTs[par][:, m, k], btm[:, k, 2 * BW + h * NAD:2 * BW + (h + 1) * NAD],
                                              start=(k == 0), stop=(k == NT - 1))
                        last.then_inc(mb[4].full, 1)

                    def d_prep():
                        for t in range(NT):
                            pe.wait_ge(*released(("pj", "d", 3)))
                            pe.wait_ge(*room(mb[t], ("mt", t)))
                            turn4(mb[t], [dtm[:, t, k * P:(k + 1) * P] for k in range(4)])
                        for t in range(NT):
                            pe.wait_ge(*released(("mt", t)))
                            for par in range(2):
                                b, r = mb[2 + par], rows_of(par)
                                pe.wait_ge(*room(b, ("mqk", t, par)))
                                for m in range(2):
                                    last = mm(b.t[:, m * P:(m + 1) * P], mqk_T[r, t, m], mqk_T[r, t, 2 + m], start=True, stop=True)
                                last.then_inc(b.full, 1)

                    def d_rows(s):
                        j = s % 2
                        pe.wait_ge(diag2_ready, s + 1)
                        pe.wait_ge(*room(mb[j], ("a", s)))
                        mm(mb[j].t[:, :], ones, prob[:, j].rearrange("p g n -> p (g n)"), start=True, stop=True).then_inc(mb[j].full, 1)

                    def d_turn(s):
                        j = s % 2
                        pe.wait_ge(scaled_d, 2 * s + 1)
                        pe.wait_ge(*room(mb[2 + j], ("mqt", s)))
                        flat = mq[:, s].rearrange("p h n -> p (h n)")
                        turn4(mb[2 + j], [flat[:, k * P:(k + 1) * P] for k in range(2)])
                        pe.wait_ge(s_ready, s + 1)
                        pe.wait_ge(*room(mb[j], ("ms", s)))
                        turn4(mb[j], [mS[:, s, h] for h in range(H)])

                    def d_scan(s):
                        t, w = TILE_OF[s], HD + 1
                        pe.wait_ge(*released(("ms", s)))
                        pe.wait_ge(*released(("mqt", s)))
                        pe.wait_ge(ones_ready, 1)
                        if s > 0:
                            pe.wait_ge(*released(("mkv", s - 1, 1)))
                        for par in range(2):
                            b, r = mb[par], rows_of(par)
                            pe.wait_ge(*room(b, ("num", s, par)))
                            for m in range(2):
                                o = b.t[:, m * w:(m + 1) * w]
                                if s > 0:
                                    for half in range(2):
                                        mm(o[rows_of(half)], mqT[r, s, m, rows_of(half)], cst[r, half ^ KIND_OF[s], m],
                                           start=True, stop=False, skip_group_check=True)
                                last = mm(o, mS[:, s, 2 * m + par], vaug[:, t, 2 * m + par], start=(s == 0), stop=True, skip_group_check=True)
                            last.then_inc(b.full, 1)
                        if s == STEPS - 1:
                            return
                        pe.wait_ge(scaled_d, 2 * s + 2)
                        for d in range(2):
                            b, r = mb[2 + d], rows_of(half_of(d, s))
                            pe.wait_ge(*room(b, ("mkv", s, d)))
                            for m in range(2):
                                for par in range(2):
                                    last = mm(b.t[rows_of(par), m * w:(m + 1) * w], wk[r, s, 2 * m + par], vaug[r, t, 2 * m + par], start=True, stop=True)
                            last.then_inc(b.full, 1)

                    def branch(n, c):
                        pe.wait_ge(y_split, BRANCHES.index(n) + 1)
                        banks = product_banks[("branch", n, c)]
                        for u in range(UN):
                            half, k0 = u // 2, (u % 2) * UK
                            unit = UN * block_no[("branch", (n, c))] + u
                            pe.wait_ge(w_split, unit + 1)
                            for t in range(NT):
                                if u == 0:
                                    pe.wait_ge(*room(banks[t], ("branch", n, c, t)))
                                for k in range(UK):
                                    w = [v[:, unit % PARTS, k] for v in (w_high, w_low)]
                                    y = [v[:, k0 + k, t * P:(t + 1) * P] for v in (y_high, y_low)]
                                    last = split_product(banks[t].t[:, half * WB:(half + 1) * WB], y, w, k0 + k == 0, k0 + k == BK - 1)
                            last.then_inc(weights_used, 1)

                    def merged_turn(q):
                        pe.wait_ge(merge_done, 10 + 2 * q)
                        for t in range(NT):
                            b = mb[2 * t + q]
                            pe.wait_ge(*room(b, ("mT", t, q)))
                            turn4(b, [merged[:, q, t, k * P:(k + 1) * P] for k in range(4)])

                    run(norm=norm, gatecols=gatecols, gatecols_turn=gatecols_turn, proj=proj, a_turn=a_turn, a_qkt=a_qkt, a_kkqk=a_kkqk, cols=cols, rows=rows, solve0=solve0,
                        t1=t1, update=update, uw=uw, scan_v=scan_v, scan_o=scan_o,
                        a_out=lambda t: y_turn("a", t, mb[t], 0), c_out=lambda t: y_turn("c", t, mb[5], 2),
                        b_out=lambda t: y_turn("b", t, mb[5], 1), d_out=lambda t: y_turn("d", t, mb[4], 3),
                        c_qkt=c_qkt, c_score=c_score, c_turn=c_turn, c_mix=c_mix, b_bias=b_bias, b_turn_in=b_turn_in, b_score=b_score,
                        b_turn=b_turn, b_mix=b_mix, d_prep=d_prep, d_rows=d_rows, d_turn=d_turn, d_scan=d_scan, branch=branch, merge_turn=merged_turn)

                @block.sync
                def _(sp):
                    def load_unit(unit):
                        kind, arg, col = plan[unit // UN]
                        u = unit % UN
                        if unit >= RAW:
                            sp.wait_ge(w_split, unit - RAW + 1)
                        if kind == "branch":
                            src, k0, col = w_branch[layer, arg[0]], (u % 2) * UK, col + (u // 2) * WB
                        else:
                            src, k0 = (w_out if kind == "out" else w_in)[layer], u * UK
                        src = src[k0 * P:(k0 + UK) * P].rearrange("(k p) n -> p k n", p=P)
                        sp.dma_start(ring[:, unit % RAW], src[:, :, col:col + WB]).then_inc(ring_full[unit % RAW], 16)

                    sp.dma_start(rawp[0:CONV * CB, :], conv_a[layer].rearrange("j (b c) -> (j b) c", c=P)).then_inc(colp_in, 16)
                    sp.dma_start(rawp[CONV * CB:CONV * CB + KT, :], norm_g[layer].rearrange("(k c) -> k c", c=P)).then_inc(colp_in, 16)
                    for unit in range(RAW):
                        load_unit(unit)
                    for unit in range(RAW, UN * len(plan)):
                        if unit == UN * block_no[("za", 0)]:
                            for t in range(NT):
                                for half in range(2):
                                    c = CHUNKS[t][half]
                                    sp.dma_start(out[0, c * C:c * C + C, :], x[rows_of(half), t, :]).then_inc(x_saved, 16)
                        if unit == UN * block_no[("gate", (BRANCHES[3], 1, 0))]:
                            sp.wait_ge(x_saved, 64)
                            sp.wait_ge(*filled(("y", "b", 1)))
                            for t in range(NT):
                                for half in range(2):
                                    c = CHUNKS[t][half]
                                    sp.dma_start(x[rows_of(half), t, :], out[0, c * C:c * C + C, :]).then_inc(x_back, 16)
                        load_unit(unit)

                @block.scalar
                def _(act):
                    f = nc.scalar.activation

                    def split(u):
                        act.wait_ge(ring_full[u % RAW], 16 * (u // RAW + 1))
                        if u >= PARTS:
                            act.wait_ge(weights_used, u - PARTS + 1)
                        f(r32(w_high[:, u % PARTS]), ring[:, u % RAW], ACT.Copy).then_inc(w_rounded, 1)

                    def take(key, dst, view, scale=1.0):
                        act.wait_ge(*filled(key))
                        f(dst, view(bank_of(key).t), ACT.Copy, scale=scale).then_inc(bank_of(key).free, 1)

                    def four(t):
                        return t.rearrange("p (k n) -> p k n", k=4)

                    def two(t):
                        return t.rearrange("p (k n) -> p k n", k=2)

                    def norm():
                        act.wait_ge(*filled("colp"))
                        f(colp, mb[4].t[:, 0:CONV * CB + KT], ACT.Copy).then_inc(mb[4].free, 1)
                        split(0)
                        for q in range(2):
                            for t in range(NT):
                                if q == 1:
                                    split(t + 1)
                                act.wait_ge(*released(("hT", t, q)))
                                v = (slice(None), slice(4 * q, 4 * q + 4), slice(t * P, (t + 1) * P))
                                f(r32(h_high[v]), h_raw[v], ACT.Copy).then_inc(h_rounded, 1)
                        split(3)
                        act.wait_ge(cols_in, 32)
                        f(r32(small_parts[0][:, 0:KT * 32]), w_small.rearrange("p k n -> p (k n)"), ACT.Copy).then_inc(small_rounded, 1)

                    def x_squares():
                        for t in range(NT):
                            f(xh[:, t], x[:, t], ACT.Square, accum_out=ssx[:, t:t + 1]).then_inc(x_squared, 1)

                    def proj(kind, arg):
                        key = ("pj", kind, arg)
                        b = bank_of(key)
                        if kind == "out":
                            return
                        act.wait_ge(*products_done(kind, arg))
                        if kind == "conv":
                            src = b.t.rearrange("p (b c n) -> p b c n", b=2, c=STEPS)
                            dst = cin[:, 2 * arg:2 * arg + 2, 2:2 + S].rearrange("p b (c n) -> p b c n", c=STEPS)
                            f(dst[:, :, 0:4:3], src[:, :, 0:2], ACT.Copy)
                            f(dst[:, :, 1:3], src[:, :, 2:4], ACT.Copy).then_inc(b.free, 1)
                            return
                        cols = slice(arg * WB, (arg + 1) * WB) if kind != "gate" else slice(arg[2] * WB, (arg[2] + 1) * WB)
                        if kind[0] == "z":
                            f(z["abcd".index(kind[1])][:, :, cols], two(b.t), ACT.Tanh, scale=0.5).then_inc(z_tanh, 1)
                        elif kind == "o":
                            if arg == 0:
                                act.wait_ge(*released(("y", "c", 1)))
                            f(og[:, :, cols], two(b.t), ACT.Tanh, scale=0.5).then_inc(b.free, 1)
                        elif kind == "gate":
                            i = branch_no[arg[:2]]
                            if i >= 2:
                                n, c = branch_list[i - 2]
                                act.wait_ge(*released(("branch", n, c, 1)))
                                if n != BRANCHES[0]:
                                    act.wait_ge(merge_done, NT * (i - 4) + 2)
                            f(gact[i % 2][:, :, cols], two(b.t), ACT.Tanh, scale=0.5).then_inc(b.free, 1)
                        elif kind == "c":
                            if arg == 0:
                                act.wait_ge(*released(("hT", 1, 1)))
                            take_pj(b, ctm[:, :, cols], two(b.t))
                        elif kind == "b":
                            if arg == 0:
                                act.wait_ge(x_saved, 64)
                            take_pj(b, btm[:, :, cols], two(b.t))
                        elif arg < 2:
                            if arg == 0:
                                act.wait_ge(*released(("y", "c", 1)))
                            take_pj(b, dtm[:, :, cols], two(b.t))
                        else:
                            h = 2 * (arg - 2)
                            take_pj(b, vaug[:, :, h:h + 2, 0:HD], b.t.rearrange("p (t h n) -> p t h n", t=NT, h=2))

                    def y_parts(n):
                        act.wait_ge(*released(("y", "abcd"[n], 1)))
                        if n != BRANCHES[0]:
                            act.wait_ge(*products_done("branch", (BRANCHES[BRANCHES.index(n) - 1], 1)))
                        f(r32(y_high), yT[n], ACT.Copy).then_inc(y_rounded, 1)

                    def take_pj(b, dst, src):
                        f(dst, src, ACT.Copy).then_inc(b.free, 1)

                    def gatecols():
                        take("small", small_T[0:32], lambda b: b[0:32, 0:S])
                        act.wait_ge(*filled("rpb"))
                        f(rpbT[0:RPB_C], mb[5].t[0:RPB_C, 0:NAH * 7], ACT.Copy).then_inc(mb[5].free, 1)

                    def gatecols_turn():
                        act.wait_ge(*released("gatecols"))
                        f(raw[:, :, 2], gps[:, :, 8:16], ACT.Tanh, scale=0.5).then_inc(gate_exp, 1)
                        act.wait_ge(params_in, 16 * PARAMS)
                        f(coef[:, 0], g_gate[:, 2], ACT.Exp).then_inc(gate_exp, 1)
                        act.wait_ge(softplus_in, 1)
                        f(softp, softp, ACT.Exp).then_inc(gate_exp, 1)
                        act.wait_ge(gate_exp, 3)
                        f(softp, softp, ACT.Ln, bias=1.0).then_inc(gate_exp, 1)

                    def conv(i):
                        if i == 0:
                            act.wait_ge(padded, 2)
                            act.wait_ge(*released("colp"))
                        else:
                            act.wait_ge(conv_out_odd, i)
                        act.wait_ge(*released(("pj", "conv", i)))
                        b = 2 * i + 1
                        for j in range(CONV):
                            last = f(taps[:, j], cin[:, b, j:j + S], ACT.Copy, scale=colp[:, j * CB + b:j * CB + b + 1])
                        last.then_inc(taps_ready, 1)

                    def silu(i):
                        act.wait_ge(conv_out, i + 1)
                        act.wait_ge(conv_out_odd, i + 1)
                        f(cin[:, 2 * i:2 * i + 2, 0:S], cac[:, 2 * i:2 * i + 2], ACT.Tanh, scale=0.5).then_inc(conv_act, 1)

                    def cols():
                        act.wait_ge(*filled("cols"))
                        flat = "p w s e -> p (w s e)"
                        f(cc.rearrange(flat), mb[5].t[:, 0:P], ACT.Copy).then_inc(mb[5].free, 1)
                        act.wait_ge(*released("cols"))
                        f(ex.rearrange(flat), cc.rearrange(flat), ACT.Exp).then_inc(sums_ready, 1)

                    def a_turn(q):
                        for t in range(NT):
                            take(("tm", t, q), tm[:, t, q * 512:(q + 1) * 512], lambda b: b)

                    def a_norm():
                        for t in range(NT):
                            act.wait_ge(*released(("tm", t, 1)))
                            sq = st.rearrange("p d h n -> p (d h n)")
                            if t:
                                act.wait_ge(summed_a, 1)
                            f(sq, tm[:, t, 0:1024], ACT.Square).then_inc(squared_a, 1)

                    def a_qkt():
                        for t in range(NT):
                            for q in range(2):
                                take(("qkt", t, q), qkt[:, 4 * q:4 * q + 4, t * P:(t + 1) * P], four)

                    def a_kkqk():
                        for t in range(NT):
                            for w in range(2):
                                take(("kkqk", t, w), kkqk[:, t, w], four)

                    def rows(s):
                        act.wait_ge(decay_arg, s + 1)
                        f(st[:, s % 2], st[:, s % 2], ACT.Exp, scale=-1.0).then_inc(decay_ready, 1)

                    def solve0(s):
                        j = s % 2
                        if s >= 2:
                            act.wait_ge(lm_ready, solve_no(s - 2, LEVELS - 1) + 1)
                        take(("lt", s), sLT[:, j], four)
                        take(("qkdt", s), qkd[:, s], four)

                    def t1(s, n):
                        take(("t1", s, n), sT1[:, s % 2], four)

                    def uw(s):
                        take(("u", s), us[:, s], four)
                        take(("w", s), lw[:, s], four)
                        take(("qd", s), qdT[:, s % 2], four)

                    def scan_o(s):
                        take(("o", s), us[:, s], four)

                    def a_sum():
                        for t in range(NT):
                            act.wait_ge(y_summed, sum_no["a"] + t + 1)
                            f(o_sq["a"][t], o_sum["a"][t], ACT.Square).then_inc(squared_y, 1)

                    def d_sum():
                        for t in range(NT):
                            act.wait_ge(y_summed, sum_no["d"] + t + 1)
                            f(o_sq["d"][t], o_sum["d"][t], ACT.Square).then_inc(squared_y, 1)

                    def y_out(name, t):
                        take(("y", name, t), yT["abcd".index(name)][:, :, t * P:(t + 1) * P], four)

                    def c_prep():
                        act.wait_ge(*released(("pj", "c", 3)))
                        f(crp[:, :, :], ctm[:, :, 0:768], ACT.Square).then_inc(squared_c, 1)

                    def c_qkt():
                        for t in range(NT):
                            take(("cq", t), cqT[:, 0:4, t * P:(t + 1) * P], four)
                            take(("ck", t), cqT[:, 4:6, t * P:(t + 1) * P], lambda b: two(b[:, 0:256]))

                    def c_score(t, q):
                        act.wait_ge(c_max, group_no(t, q) + 1)
                        b = bank_of(("cs", t, q))
                        if group_no(t, q) >= 2:
                            act.wait_ge(*filled(("cp", t - 1, q)))
                        for m in range(2):
                            h = 2 * q + m
                            last = f(prob[:, q, m], b.t[:, m * S:(m + 1) * S], ACT.Exp, scale=HD ** -0.5, bias=nmc[:, t, h:h + 1],
                                     accum_out=smc[:, t, h:h + 1])
                        last.then_inc(b.free, 1)

                    def c_turn(t, q):
                        if group_no(t, q) >= 1:
                            act.wait_ge(*filled(("co", (group_no(t, q) - 1) // 2, 1 - q)))
                        take(("cp", t, q), probT.rearrange("p g k n -> p (g k n)"), lambda b: b)

                    def b_square():
                        act.wait_ge(*released(("y", "c", 1)))
                        for t in range(NT):
                            f(gact[t].rearrange("p t n -> p (t n)"), btm[:, t, 0:1024], ACT.Square).then_inc(squared_b, 1)

                    def b_turn_in():
                        for t in range(NT):
                            for w in range(2):
                                take(("nqk", t, w), (nqT, nkT)[w][:, :, t * P:(t + 1) * P], four)

                    def b_score(t, q):
                        for par in range(2):
                            act.wait_ge(b_max, 2 * group_no(t, q) + par + 1)
                            for m in range(2):
                                h = 4 * q + 2 * m + par
                                last = f(b_probs[q][:, par, m], b_probs[q][:, par, m], ACT.Exp, bias=nmb[:, t, h:h + 1], accum_out=smb[:, t, h:h + 1])
                            last.then_inc(b_prob, 1)

                    def b_turn(t, q):
                        for par in range(2):
                            if group_no(t, q) >= 1:
                                n = group_no(t, q) - 1
                                act.wait_ge(*filled(("bo", n // 2, n % 2)))
                            take(("bp", t, q, par), probTs[par].rearrange("p g k n -> p (g k n)"), lambda b: b)

                    def d_prep():
                        for t in range(NT):
                            take(("mt", t), mqk_T[:, t], four)
                        for t in range(NT):
                            for par in range(2):
                                take(("mqk", t, par), mqk[:, t, par:H:2], lambda b: two(b[:, 0:256]), scale=MLK ** -0.5)

                    def d_m():
                        act.wait_ge(m_args, 4)
                        f(e_out.rearrange("p k s h -> p (k s h)"), e_in.rearrange("p k s h -> p (k s h)"), ACT.Exp).then_inc(m_exp, 1)
                        f(dec.rearrange("p s k h -> p (s k h)"), dec_in.rearrange("p s k h -> p (s k h)"), ACT.Exp).then_inc(m_exp, 1)

                    def d_step(s):
                        act.wait_ge(s_arg, s + 1)
                        f(mS[:, s], mS[:, s], ACT.Exp).then_inc(s_exp, 1)

                    def d_turn(s):
                        take(("mqt", s), mqT[:, s], lambda b: two(b[:, 0:256]))
                        take(("ms", s), mS[:, s], four)

                    def d_scan(s):
                        w = HD + 1
                        for par in range(2):
                            take(("num", s, par), num[:, s, par:H:2], lambda b: two(b[:, 0:2 * w]))

                    def merged_take(q):
                        if q == 0:
                            act.wait_ge(*products_done("gate", (BRANCHES[3], 1, 1)))
                        for t in range(NT):
                            act.wait_ge(*filled(("mT", t, q)))
                            f(r32(h_high[:, 4 * q:4 * q + 4, t * P:(t + 1) * P]), four(bank_of(("mT", t, q)).t), ACT.Copy, scale=0.5)\
                                .then_inc(m_rounded, 1)

                    x_squares()
                    act.dma_start(w_small[:, :, 0:16], w_in[layer].rearrange("(k p) n -> p k n", p=P)[:, :, A_AB:A_AB + 16]).then_inc(cols_in, 16)
                    act.dma_start(w_small[:, :, 16:32], w_in[layer].rearrange("(k p) n -> p k n", p=P)[:, :, D_IF:D_IF + 16]).then_inc(cols_in, 16)
                    act.dma_start(rpb[0:NAH * RPB_R, :], na_rpb[layer].rearrange("h r c -> (h r) c")).then_inc(params_in, 16)
                    shared = [(g_dn, dn_norm_g[layer]), (g_ml, ml_norm_g[layer]), (g_nq, na_q_norm[layer]), (g_nk, na_k_norm[layer]),
                              (graw[:, 0], ga_q_norm[layer]), (graw[:, 2], ga_k_norm[layer])]
                    for dst, src in shared:
                        act.dma_start(dst, src[None, :].to_broadcast([P, src.shape[0]])).then_inc(params_in, 16)
                    for k, src in enumerate((dn_dt_bias, ml_f_bias, dn_a_log, ml_i_bias)):
                        src = src[layer].rearrange("d h -> (d h)")
                        act.dma_start(g_gate[:, k], src[None, :].to_broadcast([P, 8])).then_inc(params_in, 16)
                    run(split=split, y_parts=y_parts, norm=norm, proj=proj, gatecols=gatecols, gatecols_turn=gatecols_turn, conv=conv, silu=silu, cols=cols, a_turn=a_turn, a_norm=a_norm, a_qkt=a_qkt, a_kkqk=a_kkqk,
                        rows=rows, solve0=solve0, t1=t1, uw=uw, scan_o=scan_o, a_sum=a_sum, d_sum=d_sum,
                        a_out=lambda t: y_out("a", t), b_out=lambda t: y_out("b", t), c_out=lambda t: y_out("c", t),
                        d_out=lambda t: y_out("d", t), c_prep=c_prep, c_qkt=c_qkt, c_score=c_score, c_turn=c_turn, b_square=b_square, b_turn_in=b_turn_in,
                        b_score=b_score, b_turn=b_turn, d_prep=d_prep, d_m=d_m, d_step=d_step, d_turn=d_turn, d_scan=d_scan, merged=merged_take)

                @block.vector
                def _(dve):
                    tt, ts, stt, reduce = nc.vector.tensor_tensor, nc.vector.tensor_scalar, nc.vector.scalar_tensor_tensor, nc.vector.tensor_reduce
                    chain = [0]

                    def mark(ins):
                        chain[0] += 1
                        ins.then_inc(dve_chain, 1)
                        return chain[0]

                    def link(ins):
                        dve.wait_ge(dve_chain, mark(ins))

                    def four(t):
                        return t.rearrange("p (k n) -> p k n", k=4)

                    def two(t):
                        return t.rearrange("p (k n) -> p k n", k=2)

                    def split(u):
                        dve.wait_ge(w_rounded, u + 1)
                        tt(r32(w_low[:, u % PARTS]), ring[:, u % RAW], w_high[:, u % PARTS], ALU.subtract).then_inc(w_split, 1)

                    def norm():
                        nc.vector.memset(cin[:, :, 0:2], 0.0).then_inc(padded, 1)
                        nc.vector.memset(cin[:, :, 2 + S:4 + S], 0.0).then_inc(padded, 1)
                        dve.wait_ge(padded, 2)
                        dve.wait_ge(rms_x, 1)
                        for t in range(NT):
                            ts(xh[:, t], x[:, t], rsx[:, t:t + 1], None, ALU.mult).then_inc(h_ready, 1)
                        dve.wait_ge(*released("colp"))
                        def low(n):
                            t, q = n % 2, n // 2
                            dve.wait_ge(h_rounded, n + 1)
                            v = (slice(None), slice(4 * q, 4 * q + 4), slice(t * P, (t + 1) * P))
                            tt(r32(h_low[v]), h_raw[v], h_high[v], ALU.subtract).then_inc(h_split, 1)

                        def scale(n):
                            t, q = n % 2, n // 2
                            dve.wait_ge(*filled(("hT", t, q)))
                            b = bank_of(("hT", t, q))
                            k0 = CONV * CB + 4 * q
                            tt(h_raw[:, 4 * q:4 * q + 4, t * P:(t + 1) * P], four(b.t), along(colp[:, k0:k0 + 4], P), ALU.mult).then_inc(b.free, 1)

                        scale(0)
                        scale(1)
                        split(0)
                        low(0)
                        low(1)
                        scale(2)
                        scale(3)
                        split(1)
                        low(2)
                        split(2)
                        low(3)
                        split(3)
                        dve.wait_ge(table_in, 16)
                        dve.wait_ge(small_rounded, 1)
                        for v in small_parts:
                            ts(r32(v[:, KT * 32:]), K("half0")[:, 0:96], 0.0, None, ALU.mult).then_inc(small_split, 1)
                        flat_small = w_small.rearrange("p k n -> p (k n)")
                        tt(r32(small_parts[1][:, 0:KT * 32]), flat_small, small_parts[0][:, 0:KT * 32], ALU.subtract).then_inc(small_split, 1)

                    def gatecols_turn():
                        b = mb[5]
                        dve.wait_ge(*filled("gatecols"))
                        nc.vector.tensor_copy(gps.rearrange("p t e -> p (t e)"), b.t[:, 0:64]).then_inc(b.free, 1)
                        dve.wait_ge(*released("gatecols"))
                        dve.wait_ge(params_in, 16 * PARAMS)
                        tt(raw[:, :, 0], gps[:, :, 0:8], over(g_gate[:, 0], NT), ALU.add)
                        stt(raw[:, :, 1], gps[:, :, 24:32], -1.0, over(g_gate[:, 1], NT), ALU.mult, ALU.subtract)
                        link(tt(raw[:, :, 3], gps[:, :, 16:24], over(g_gate[:, 3], NT), ALU.add))
                        for k in range(2):
                            last = stt(softp[:, :, k], raw[:, :, k], -1.0, raw[:, :, k], ALU.mult, ALU.min)
                            if k == 0:
                                link(last)
                        last.then_inc(softplus_in, 1)
                        dve.wait_ge(gate_exp, 2)
                        ts(coef[:, 0], coef[:, 0], -1.0, None, ALU.mult)
                        nc.vector.memset(coef[:, 1], -1.0)
                        link(ts(raw[:, :, 2], raw[:, :, 2], 0.5, 0.5, ALU.mult, ALU.add))
                        dve.wait_ge(gate_exp, 4)
                        for k in range(2):
                            link(stt(softp[:, :, k], raw[:, :, k], 0.0, softp[:, :, k], ALU.max, ALU.add))
                        for k in range(2):
                            tt(raw[:, :, k], softp[:, :, k], over(coef[:, k], NT), ALU.mult).then_inc(gates_ready, 1)

                    def conv(i):
                        dve.wait_ge(*released(("pj", "conv", i)))
                        b = 2 * i
                        for j in range(CONV):
                            w = colp[:, j * CB + b:j * CB + b + 1]
                            if j == 0:
                                link(ts(cac[:, b], cin[:, b, 0:S], w, None, ALU.mult))
                            elif j < CONV - 1:
                                link(stt(cac[:, b], cin[:, b, j:j + S], w, cac[:, b], ALU.mult, ALU.add))
                            else:
                                stt(cac[:, b], cin[:, b, j:j + S], w, cac[:, b], ALU.mult, ALU.add).then_inc(conv_out, 1)

                    def silu(i):
                        dve.wait_ge(conv_act, i + 1)
                        for b in range(2 * i, 2 * i + 2):
                            a = cin[:, b, 0:S].rearrange("p (c n) -> p c n", c=STEPS)
                            v = cac[:, b].rearrange("p (c n) -> p c n", c=STEPS)
                            o = csl[:, b].rearrange("p (c n) -> p c n", c=STEPS)
                            for t, sl in ((0, slice(0, 4, 3)), (1, slice(1, 3))):
                                stt(o[:, 2 * t:2 * t + 2], a[:, sl], 1.0, v[:, sl], ALU.add, ALU.mult).then_inc(silu_ready, 1)

                    def cols():
                        dve.wait_ge(selected, 8)
                        dve.wait_ge(sums_ready, 1)
                        ts(hbeta, sel[:, :, 2], 0.5, None, ALU.mult).then_inc(terms_ready, 1)
                        tt(bev, sel[:, :, 2], ex[:, 0, :, 0:H], ALU.mult).then_inc(terms_ready, 1)
                        tt(av, sel[:, :, 3], cc[:, 0, :, H:8], ALU.subtract).then_inc(terms_ready, 1)

                    def a_norm():
                        sq = st.rearrange("p d h n -> p (d h) n")
                        for t in range(NT):
                            dve.wait_ge(squared_a, t + 1)
                            reduce(ssa[:, t], sq, X, ALU.add).then_inc(summed_a, 1)

                    def a_scale():
                        dve.wait_ge(rms_a, 1)
                        for t in range(NT):
                            v = tm[:, t, 0:1024].rearrange("p (g n) -> p g n", g=8)
                            tt(v, v, along(rsa[:, t], P), ALU.mult).then_inc(normed_a, 1)

                    def rows(s):
                        j, kind, t = s % 2, KIND_OF[s], TILE_OF[s]
                        dve.wait_ge(*filled(("gc", s)))
                        b = bank_of(("gc", s))
                        if s == 0:
                            dve.wait_ge(*released(("kkqk", 1, 1)))
                            dve.wait_ge(table_in, 16)
                        if s >= 2:
                            dve.wait_ge(decay_beta, s - 1)
                        tt(st[:, j], four(b.t), along(cc[:, 0, s, 0:H], P), ALU.subtract).then_inc(b.free, 1)
                        dve.wait_ge(*released(("gc", s)))
                        stt(st[:, j], st[:, j], 0.0, over(K(f"mask{kind}"), H), ALU.max, ALU.subtract).then_inc(decay_arg, 1)
                        dve.wait_ge(decay_ready, s + 1)
                        tt(qkd[:, s], st[:, j], kkqk[:, t, 1], ALU.mult)
                        dve.wait_ge(decay_beta, s + 1)
                        tt(lw[:, s], vk[:, j], kkqk[:, t, 0], ALU.mult).then_inc(l_ready, 1)

                    def solve0(s):
                        j, kind = s % 2, KIND_OF[s]
                        dve.wait_ge(*released(("lt", s)))
                        link(tt(halves(sXT[:, j]), halves(sLT[:, j]), over(K(f"level{1 - kind}_0"), 2 * H), ALU.mult))
                        tt(sXT[:, j], over(ident, H), sXT[:, j], ALU.subtract).then_inc(xt0_ready, 1)

                    def update(s, n):
                        j = s % 2
                        if n < LEVELS - 1:
                            b = bank_of(("dx", s, n))
                            dve.wait_ge(*filled(("dx", s, n)))
                            tt(sX[:, j], sX[:, j], four(b.t), ALU.subtract).then_inc(b.free, 1)
                        b = bank_of(("dxt", s, n))
                        dve.wait_ge(*filled(("dxt", s, n)))
                        tt(sXT[:, j], sXT[:, j], four(b.t), ALU.subtract).then_inc(b.free, 1)

                    def scan_v(s):
                        dve.wait_ge(*released(("u", s)))
                        if s == 0:
                            nc.vector.tensor_copy(vn, us[:, 0]).then_inc(vn_ready, 1)
                            return
                        dve.wait_ge(*filled(("ws", s)))
                        tt(vn, us[:, s], four(mb[4].t), ALU.subtract).then_inc(mb[4].free, 1)

                    def scan_o(s):
                        if s == STEPS - 1:
                            return
                        for d in range(2):
                            b = mb[4 + d]
                            dve.wait_ge(*filled(("kv", s, d)))
                            if s == 0:
                                nc.vector.tensor_copy(st[:, d], four(b.t)).then_inc(b.free, 1)
                            else:
                                dve.wait_ge(st_decayed, 2 * (s - 1) + d + 1)
                                tt(st[:, d], st[:, d], four(b.t), ALU.add).then_inc(b.free, 1)

                    def sum_square(name, pairs):
                        for t, (a, b) in enumerate(pairs):
                            tt(o_sum[name][t], a, b, ALU.add).then_inc(y_summed, 1)
                        for t in range(NT):
                            dve.wait_ge(squared_y, sum_no[name] + t + 1)
                            reduce(sso[:, t + (2 if name == "d" else 0)], o_sq[name][t], X, ALU.add).then_inc(summed_y, 1)

                    def a_sum():
                        dve.wait_ge(*released(("o", STEPS - 1)))
                        sum_square("a", ((us[:, 0], us[:, 3]), (us[:, 1], us[:, 2])))

                    def gain_z(b, gain):
                        v = z[b].rearrange("p t (h n) -> p t h n", h=H)
                        for t in range(NT):
                            mark(tt(v[:, t], v[:, t], over(gain, H), ALU.mult))

                    def norm_gate(name, t, factor):
                        o = o_sum[name][t]
                        dve.wait_ge(rms_y, sum_no[name] // NT + 1)
                        link(tt(o, o, along(rso[:, t + (2 if name == "d" else 0)], HD), ALU.mult))
                        gate_y(name, t, factor)

                    def gate_y(name, t, factor):
                        y = y_tile[name][t]
                        stt(y, y, factor, z["abcd".index(name)][:, t], ALU.mult, ALU.mult).then_inc(y_ready, 1)

                    def a_gate(t):
                        norm_gate("a", t, 0.5)

                    def d_gate(t):
                        norm_gate("d", t, 0.25)

                    def z_gate(kind, i):
                        b = bank_of(("pj", kind, i))
                        dve.wait_ge(z_tanh, z_no[(kind, i)] + 1)
                        v = z["abcd".index(kind[1])][:, :, i * WB:(i + 1) * WB]
                        stt(v, v, 1.0, two(b.t), ALU.add, ALU.mult).then_inc(b.free, 1)

                    def proj(kind, arg):
                        if kind[0] == "z":
                            z_gate(kind, arg)
                            if kind == "za" and arg == 1:
                                dve.wait_ge(*released(("pj", kind, arg)))
                                dve.wait_ge(params_in, 16 * PARAMS)
                                gain_z(0, g_dn)
                        if kind == "out":
                            b = bank_of(("pj", kind, arg))
                            if arg == 0:
                                dve.wait_ge(x_back, 64)
                            dve.wait_ge(*products_done(kind, arg))
                            v = x[:, :, arg * WB:(arg + 1) * WB]
                            tt(v, v, two(b.t), ALU.add).then_inc(b.free, 1)

                    def y_parts(n):
                        dve.wait_ge(y_rounded, BRANCHES.index(n) + 1)
                        tt(r32(y_low), yT[n], y_high, ALU.subtract).then_inc(y_split, 1)

                    def c_prep():
                        dve.wait_ge(squared_c, 1)
                        reduce(ssc.rearrange("p t g -> p (t g)"), crp.rearrange("p t (g n) -> p t g n", g=6), X, ALU.add).then_inc(summed_c, 1)

                    def c_rotate(t):
                        if t == 0:
                            dve.wait_ge(summed_c, 1)
                            dve.wait_ge(rope_ready, 4)
                        swp = prob.rearrange("p j g n -> p (j g n)")[:, 0:768]
                        for h0, h1, w in ((0, 4, 0), (4, 6, 2)):
                            src = ctm[:, t, h0 * HD:h1 * HD]
                            out_ = crp[:, t, h0 * HD:h1 * HD]
                            tt(heads(out_, h1 - h0), heads(src, h1 - h0), over(rope[:, w, t], h1 - h0), ALU.mult)
                            sv = src.rearrange("p (h s n) -> p h s n", s=2, n=32)
                            dv = swp[:, h0 * HD:h1 * HD].rearrange("p (h s n) -> p h s n", s=2, n=32)
                            rv = rope[:, w + 1, t].rearrange("p (a s n) -> p a s n", a=2, s=2)
                            for a in range(2):
                                for s in range(2):
                                    sl = slice(a, 2 * (h1 - h0), 2)
                                    last = mark(tt(dv[:, sl, s], sv[:, sl, 1 - s], over(rv[:, a, s], h1 - h0), ALU.mult))
                        dve.wait_ge(dve_chain, last)
                        link(tt(crp[:, t], crp[:, t], swp, ALU.add))
                        if t == 0:
                            dve.wait_ge(rms_c, 1)
                        tt(heads(crp[:, t], 6), heads(crp[:, t], 6), along(rsc[:, t], HD), ALU.mult).then_inc(rotated, 1)

                    def c_score(t, q):
                        b = bank_of(("cs", t, q))
                        dve.wait_ge(*filled(("cs", t, q)))
                        m = nmc[:, t, 2 * q:2 * q + 2]
                        link(reduce(m, two(b.t), X, ALU.max, negate=True))
                        ts(m, m, HD ** -0.5, None, ALU.mult).then_inc(c_max, 1)

                    def c_mix(t, q):
                        b = bank_of(("co", t, q))
                        link(nc.vector.reciprocal(rmc[:, t, 2 * q:2 * q + 2], smc[:, t, 2 * q:2 * q + 2]))
                        dve.wait_ge(*filled(("co", t, q)))
                        tt(heads(crp[:, t, q * 256:(q + 1) * 256], 2), two(b.t[:, 0:256]), along(rmc[:, t, 2 * q:2 * q + 2], HD), ALU.mult)\
                            .then_inc(b.free, 1)

                    def c_sum(t):
                        dve.wait_ge(*released(("co", t, 1)))
                        gate_y("c", t, 0.5)

                    def b_sum(t):
                        dve.wait_ge(*released(("bo", t, 1)))
                        gate_y("b", t, 0.5)

                    def b_bias(i):
                        if i == 0:
                            dve.wait_ge(*filled(("w", STEPS - 1)))
                        dve.wait_ge(*filled(("bias", i)))
                        b = bank_of(("bias", i))
                        src = b.t[0:C, 0:8 * 56].rearrange("p (c h o) -> p h o c", c=8, h=NAH)
                        for t in range(NT):
                            for half in range(2):
                                r = CHUNKS[t][half]
                                dst = bias[rows_of(half), t].rearrange("p h (k c) -> p h k c", k=STEPS)[:, :, :, 8 * i:8 * i + 8]
                                win = K("window")[0:C, 8 * i:8 * i + 8][:, None, None, :].to_broadcast([C, NAH, 2, 8])
                                tt(dst[:, :, 0:2], src[:, :, 3 - r:7 - r:3], win, ALU.add)
                                last = tt(dst[:, :, 2:4], src[:, :, 4 - r:6 - r], win, ALU.add)
                        last.then_inc(b.free, 1)

                    def b_square():
                        for t in range(NT):
                            dve.wait_ge(squared_b, t + 1)
                            sq = gact[t].rearrange("p t (g n) -> p (t g) n", n=NAD)
                            reduce(ssb[:, t], sq, X, ALU.add).then_inc(summed_b, 1)

                    def b_prep():
                        dve.wait_ge(rms_b, 1)
                        for t in range(NT):
                            v = btm[:, t, 0:1024].rearrange("p (g n) -> p g n", g=16)
                            link(tt(v, v, along(rsb[:, t], NAD), ALU.mult))
                            tt(v[:, 0:NAH], v[:, 0:NAH], over(g_nq, NAH), ALU.mult).then_inc(gained_b, 1)

                    def b_score(t, q):
                        for par in range(2):
                            b = bank_of(("bs", t, q, par))
                            dve.wait_ge(*filled(("bs", t, q, par)))
                            n = group_no(t, q)
                            if n >= 2:
                                dve.wait_ge(*filled(("bp", t - 1, q, par)))
                            hs = slice(4 * q + par, 4 * q + par + 3, 2)
                            stt(b_probs[q][:, par], two(b.t), NAD ** -0.5, bias[:, t, hs], ALU.mult, ALU.add).then_inc(b.free, 1)
                            dve.wait_ge(*released(("bs", t, q, par)))
                            reduce(nmb[:, t, hs], b_probs[q][:, par], X, ALU.max, negate=True).then_inc(b_max, 1)

                    def b_mix(t, q):
                        b = bank_of(("bo", t, q))
                        dve.wait_ge(b_prob, 2 * group_no(t, q) + 2)
                        link(nc.vector.reciprocal(rmb[:, t, 4 * q:4 * q + 4], smb[:, t, 4 * q:4 * q + 4]))
                        dve.wait_ge(*filled(("bo", t, q)))
                        tt(btm[:, t, q * 256:(q + 1) * 256].rearrange("p (h n) -> p h n", h=4), four(b.t[:, 0:256]),
                           along(rmb[:, t, 4 * q:4 * q + 4], NAD), ALU.mult).then_inc(b.free, 1)

                    def d_prep():
                        dve.wait_ge(*released(("pj", "o", 1)))
                        dve.wait_ge(*released(("pj", "zd", 1)))
                        for t in range(NT):
                            last = mark(stt(z[3][:, t], og[:, t], 1.0, z[3][:, t], ALU.add, ALU.mult))
                        dve.wait_ge(dve_chain, last)
                        gain_z(3, g_ml)

                    def d_rows(s):
                        b = bank_of(("a", s))
                        dve.wait_ge(*filled(("a", s)))
                        link(tt(mS[:, s], four(b.t), over(K(f"mask{KIND_OF[s]}"), H), ALU.add))
                        reduce(amx[:, s], b.t.rearrange("p (h k n) -> p h k n", h=H, k=2), X, ALU.max).then_inc(b.free, 1)
                        mark(reduce(cm[:, s], mS[:, s], X, ALU.max))

                    def d_m():
                        link(nc.vector.memset(mst[:, 0], 0.0))
                        for s in range(STEPS):
                            link(tt(mxs[:, s], mst[:, s], amx[:, s].rearrange("p h k -> p k h"), ALU.max))
                            if s == STEPS - 1:
                                break
                            swap = KIND_OF[s] != KIND_OF[s + 1]
                            for k in range(2):
                                link(tt(mst[:, s + 1, k ^ swap], cc[:, 2 + k, s, H:8], mxs[:, s, k], ALU.add))
                        for half in range(2):
                            r = rows_of(half)
                            nc.vector.tensor_copy(msel[r], mst[r, :, half])
                            link(nc.vector.tensor_copy(mxsel[r], mxs[r, :, half]))
                        link(tt(mrun, cm, msel, ALU.max))
                        tt(e_in[:, 0], msel, mrun, ALU.subtract).then_inc(m_args, 1)
                        stt(e_in[:, 1], cc[:, 0, :, H:8], -1.0, mrun, ALU.mult, ALU.subtract).then_inc(m_args, 1)
                        tt(e_in[:, 2], av, mxsel, ALU.subtract).then_inc(m_args, 1)
                        tt(dec_in, mst, mxs, ALU.subtract).then_inc(m_args, 1)
                        dve.wait_ge(m_exp, 2)
                        ts(e_out[:, 2], e_out[:, 2], MLK ** -0.5, None, ALU.mult).then_inc(m_terms, 1)

                    def d_step(s):
                        tt(mS[:, s], mS[:, s], along(mrun[:, s], P), ALU.subtract).then_inc(s_arg, 1)
                        dve.wait_ge(s_exp, s + 1)
                        dve.wait_ge(*released(("mqk", 1, 1)))
                        tt(mS[:, s], mS[:, s], mqk[:, TILE_OF[s]], ALU.mult).then_inc(s_ready, 1)

                    def d_scan(s):
                        if s == STEPS - 1:
                            return
                        for d in range(2):
                            b = mb[2 + d]
                            v = two(b.t[:, 0:2 * (HD + 1)])
                            dve.wait_ge(*filled(("mkv", s, d)))
                            if s == 0:
                                nc.vector.tensor_copy(cst[:, d], v).then_inc(b.free, 1)
                            else:
                                dve.wait_ge(c_decayed, 2 * (s - 1) + d + 1)
                                tt(cst[:, d], cst[:, d], v, ALU.add).then_inc(b.free, 1)

                    def d_den():
                        dve.wait_ge(*released(("num", STEPS - 1, 1)))
                        v = num[:, :, :, HD]
                        link(stt(nden, v, -1.0, v, ALU.mult, ALU.max))
                        link(tt(nden, nden, e_out[:, 1], ALU.max))
                        link(nc.vector.reciprocal(den, nden))
                        for s in range(STEPS):
                            o = num[:, s, :, 0:HD]
                            last = mark(tt(o, o, along(den[:, s], HD), ALU.mult))
                        dve.wait_ge(dve_chain, last)

                    def d_sum():
                        sum_square("d", [(num[:, a, :, 0:HD], num[:, b, :, 0:HD]) for a, b in ((0, 3), (1, 2))])

                    def branch(n, c):
                        i = branch_no[(n, c)]
                        dve.wait_ge(*products_done("branch", (n, c)))
                        dve.wait_ge(*released(("pj", "gate", (n, c, 1))))
                        for t in range(NT):
                            b = bank_of(("branch", n, c, t))
                            dst = merged[:, c, t] if n == BRANCHES[0] else gact[i % 2][:, t]
                            stt(dst, gact[i % 2][:, t], 1.0, b.t, ALU.add, ALU.mult).then_inc(b.free, 1)
                        if (n, c) == branch_list[-1]:
                            dve.wait_ge(merge_done, NT * (i - 2))
                            for t in range(NT):
                                dve.wait_ge(*released(("branch", n, c, t)))
                                m = merged[:, c, t]
                                tt(m, m, gact[i % 2][:, t], ALU.add).then_inc(merge_done, 1)

                    def merged_take(q):
                        for t in range(NT):
                            b = bank_of(("mT", t, q))
                            dve.wait_ge(m_rounded, 2 * q + t + 1)
                            v = (slice(None), slice(4 * q, 4 * q + 4), slice(t * P, (t + 1) * P))
                            stt(r32(h_low[v]), four(b.t), 0.5, h_high[v], ALU.mult, ALU.subtract).then_inc(b.free, 1)

                    run(split=split, y_parts=y_parts, merged=merged_take, norm=norm, gatecols_turn=gatecols_turn, conv=conv, silu=silu, cols=cols, a_norm=a_norm, a_scale=a_scale, rows=rows, solve0=solve0, update=update, scan_v=scan_v,
                        scan_o=scan_o, a_sum=a_sum, a_gate=a_gate, d_gate=d_gate, proj=proj, c_prep=c_prep, c_rotate=c_rotate, c_score=c_score, c_mix=c_mix,
                        c_sum=c_sum, b_sum=b_sum, b_bias=b_bias, b_square=b_square, b_prep=b_prep, b_score=b_score, b_mix=b_mix, d_prep=d_prep,
                        d_rows=d_rows, d_m=d_m, d_step=d_step, d_scan=d_scan, d_den=d_den, d_sum=d_sum, branch=branch)

                @block.gpsimd
                def _(pool):
                    chain = [0]

                    def link(ins):
                        chain[0] += 1
                        ins.then_inc(pool_chain, 1)
                        pool.wait_ge(pool_chain, chain[0])

                    def rstd(dst, src, scale, n, signal):
                        link(pool.tensor_scalar(dst, src, scale, EPS, ALU.mult, ALU.add))
                        pool.tensor_tensor(dst, dst, neg_half[:, 0:n], ALU.pow).then_inc(signal, 1)

                    def norm():
                        pool.wait_ge(x_squared, NT)
                        rstd(rsx, ssx, 1.0 / D, NT, rms_x)

                    def conv(i):
                        b = 2 * i + 1
                        pool.wait_ge(taps_ready, i + 1)
                        pool.tensor_tensor(taps[:, 0], taps[:, 0], taps[:, 1], ALU.add)
                        link(pool.tensor_tensor(taps[:, 2], taps[:, 2], taps[:, 3], ALU.add))
                        link(pool.tensor_tensor(taps[:, 0], taps[:, 0], taps[:, 2], ALU.add))
                        pool.tensor_tensor(cac[:, b], taps[:, 0], taps[:, 4], ALU.add).then_inc(conv_out_odd, 1)
                        pool.wait_ge(conv_out_odd, i + 1)

                    def cols():
                        pool.wait_ge(gates_ready, 2)
                        for s in range(STEPS):
                            for half in range(2):
                                d = half ^ KIND_OF[s]
                                pool.tensor_copy(sel[rows_of(half), s], raw[rows_of(half), TILE_OF[s], :, d * H:d * H + H]).then_inc(selected, 1)

                    def a_norm():
                        pool.wait_ge(summed_a, NT)
                        fr = rsa.rearrange("p t g -> p (t g)")
                        pool.tensor_scalar(rsa[:, :, 0:H], ssa[:, :, 0:H], float(HD), 4 * EPS * HD, ALU.mult, ALU.add)
                        link(pool.tensor_scalar(rsa[:, :, H:8], ssa[:, :, H:8], 1.0, 4 * EPS, ALU.mult, ALU.add))
                        pool.tensor_tensor(fr, fr, neg_half[:, 0:16], ALU.pow).then_inc(rms_a, 1)

                    def diagonal(s):
                        if s == 2:
                            pool.wait_ge(*filled(("kkqk", 1, 1)))
                        pool.tensor_tensor(diag[s], over(ident, H), along(cc[:, 0, s, 0:H], P), ALU.mult).then_inc(diag_ready, 1)

                    def cols_diagonals():
                        cols()
                        pool.wait_ge(table_in, 16)
                        pool.wait_ge(sums_ready, 1)
                        diagonal(0)
                        diagonal(1)

                    def rows(s):
                        if s + 2 < STEPS:
                            diagonal(s + 2)
                        pool.wait_ge(decay_ready, s + 1)
                        if s >= 2:
                            pool.wait_ge(l_ready, s - 1)
                        pool.tensor_tensor(vk[:, s % 2], st[:, s % 2], along(sel[:, s, 2], P), ALU.mult).then_inc(decay_beta, 1)
                        if s < 2:
                            first_inverse(s)

                    def first_inverse(s):
                        j, kind = s % 2, KIND_OF[s]
                        pool.wait_ge(l_ready, s + 1)
                        if s >= 2:
                            pool.wait_ge(*filled(("w", s - 2)))
                        link(pool.tensor_tensor(halves(sX[:, j]), halves(lw[:, s]), over(K(f"level{kind}_0"), 2 * H), ALU.mult))
                        pool.tensor_tensor(sX[:, j], over(ident, H), sX[:, j], ALU.subtract).then_inc(x0_ready, 1)

                    def solve0(s):
                        if s >= 2:
                            first_inverse(s)

                    def t1(s, n):
                        j, kind = s % 2, KIND_OF[s]
                        if n == 1:
                            pool.wait_ge(*released(("lt", s)))
                        if n > 1:
                            pool.wait_ge(*filled(("t1", s, n - 1)))
                        elif s >= 2:
                            pool.wait_ge(*filled(("qd", s - 2)))
                        pool.tensor_tensor(halves(sLm[:, j]), halves(sLT[:, j]), over(K(f"level{1 - kind}_{n}"), 2 * H), ALU.mult).then_inc(lm_ready, 1)

                    def uw(s):
                        j, t = s % 2, TILE_OF[s]
                        pool.wait_ge(terms_ready, 3)
                        if s == 0:
                            pool.wait_ge(l_ready, STEPS)
                        if s >= 1:
                            pool.wait_ge(*filled(("w", s - 1)))
                        pool.tensor_tensor(vk[:, 0], heads(tm[:, t, 2 * BW:3 * BW], H), along(hbeta[:, s], P), ALU.mult).then_inc(scaled_uw, 1)
                        pool.tensor_tensor(vk[:, 1], heads(tm[:, t, BW:2 * BW], H), along(bev[:, s], P), ALU.mult).then_inc(scaled_uw, 1)
                        pool.wait_ge(*filled(("t1", s, LEVELS - 1)))
                        pool.tensor_tensor(sLm[:, j], heads(tm[:, t, 0:BW], H), along(ex[:, 0, s, 0:H], P), ALU.mult).then_inc(scaled_uw, 1)
                        if s == STEPS - 1:
                            return
                        if s >= 2:
                            pool.wait_ge(*filled(("kv", s - 2, 1)))
                        pool.tensor_tensor(kd[:, j], heads(tm[:, t, BW:2 * BW], H), along(ex[:, 1, s, 0:H], P), ALU.mult).then_inc(scaled_uw, 1)

                    def scan_o(s):
                        if 0 < s < STEPS - 1:
                            pool.wait_ge(*filled(("o", s)))
                            pool.wait_ge(*released(("kv", s - 1, 1)))
                            for d in range(2):
                                w = 2 + half_of(d, s)
                                pool.tensor_tensor(st[:, d], st[:, d], along(ex[:, w, s, 0:H], P), ALU.mult).then_inc(st_decayed, 1)

                    def sum_rms(b):
                        n, k = sum_no[b], 2 if b == "d" else 0
                        pool.wait_ge(summed_y, n + NT)
                        rstd(rso[:, k:k + NT].rearrange("p t h -> p (t h)"), sso[:, k:k + NT].rearrange("p t h -> p (t h)"), 1.0 / HD, NT * H, rms_y)

                    def make_rope():
                        pool.wait_ge(table_in, 16)
                        pool.wait_ge(params_in, 16 * PARAMS)
                        for w in (0, 2):
                            v = [graw[:, w + i].rearrange("p (a s n) -> p a s n", a=2, s=2) for i in range(2)]
                            for i in range(2):
                                last = pool.tensor_copy(v[1][:, :, i], v[0][:, :, 1 - i])
                                link(last)
                        for w in range(4):
                            src = K(("cos", "sin")[w % 2]).rearrange("p (t n) -> p t n", t=NT)
                            pool.tensor_tensor(rope[:, w], src, over(graw[:, w], NT), ALU.mult).then_inc(rope_ready, 1)

                    def c_prep():
                        pool.wait_ge(summed_c, 1)
                        rstd(rsc.rearrange("p t g -> p (t g)"), ssc.rearrange("p t g -> p (t g)"), 1.0 / HD, 12, rms_c)

                    def b_prep():
                        link(pool.tensor_tensor(g_nq, g_nq, g_nk, ALU.mult))
                        pool.wait_ge(summed_b, NT)
                        rstd(rsb.rearrange("p t g -> p (t g)"), ssb.rearrange("p t g -> p (t g)"), 1.0 / NAD, 32, rms_b)

                    def d_prep():
                        pool.wait_ge(*released(("pj", "d", 0)))
                        pool.memset(vaug[:, :, :, HD:HD + 1], 1.0).then_inc(ones_ready, 1)

                    def d_rows(s):
                        j = s % 2
                        if s == 0:
                            pool.wait_ge(*released(("y", "c", 1)))
                        if s >= 2:
                            pool.wait_ge(*filled(("a", s - 2)))
                        dg = prob[:, j].rearrange("p g n -> p (g n)")
                        pool.tensor_tensor(heads(dg, H), over(ident, H), along(av[:, s], P), ALU.mult).then_inc(diag2_ready, 1)

                    def d_m():
                        pool.wait_ge(m_exp, 2)
                        pool.wait_ge(ones_ready, 1)
                        for par in range(2):
                            pool.tensor_copy(decp[rows_of(par)], dec[rows_of(par), :, :, par:H:2]).then_inc(m_terms, 1)
                        pool.wait_ge(m_terms, 3)

                    def d_step(s):
                        t = TILE_OF[s]
                        if s == 0:
                            pool.wait_ge(*filled(("bo", 1, 1)))
                        pool.tensor_tensor(mq[:, s], heads(dtm[:, t, 0:256], H), along(e_out[:, 0, s], MLK), ALU.mult).then_inc(scaled_d, 1)
                        pool.tensor_tensor(wk[:, s], heads(dtm[:, t, 256:512], H), along(e_out[:, 2, s], MLK), ALU.mult).then_inc(scaled_d, 1)

                    def d_scan(s):
                        if 0 < s < STEPS - 1:
                            pool.wait_ge(*filled(("num", s, 1)))
                            pool.wait_ge(*released(("mkv", s - 1, 1)))
                            for d in range(2):
                                pool.tensor_tensor(cst[:, d], cst[:, d], along(decp[:, s, half_of(d, s)], HD + 1), ALU.mult).then_inc(c_decayed, 1)

                    def branch(n, c):
                        i = branch_no[(n, c)]
                        for t in range(NT):
                            if n != BRANCHES[0] and (n, c) != branch_list[-1]:
                                pool.wait_ge(*released(("branch", n, c, t)))
                                m = merged[:, c, t]
                                pool.tensor_tensor(m, m, gact[i % 2][:, t], ALU.add).then_inc(merge_done, 1)

                    run(norm=norm, rope=make_rope, conv=conv, cols=cols_diagonals, a_norm=a_norm, rows=rows, solve0=solve0, t1=t1, uw=uw, scan_o=scan_o,
                        a_sum=lambda: sum_rms("a"), d_sum=lambda: sum_rms("d"), c_prep=c_prep, b_prep=b_prep,
                        d_prep=d_prep, d_rows=d_rows, d_m=d_m, d_step=d_step, d_scan=d_scan, branch=branch)

            nums = [s.num for s in layer_sems]
            nc.all_engine_barrier()
            nc.sync.sem_clear(range(min(nums), max(nums) + 1))
            nc.all_engine_barrier()

        with nc.Block() as block:
            @block.sync
            def _(sp):
                for t in range(NT):
                    for half in range(2):
                        c = CHUNKS[t][half]
                        sp.dma_start(out[0, c * C:c * C + C, :], x[rows_of(half), t, :]).then_inc(stored, 16)
                sp.wait_ge(stored, 64)


_INS = ["x", "norm_g", "w_in", "conv_a", "dn_a_log", "dn_dt_bias", "dn_norm_g", "na_q_norm", "na_k_norm", "na_rpb",
        "ga_q_norm", "ga_k_norm", "ml_i_bias", "ml_f_bias", "ml_norm_g", "w_branch", "w_out"]


def kernel(**inputs):
    import concourse.bacc as _bacc
    from concourse.bass_utils import run_bass_kernel_spmd as _run

    nc = _bacc.Bacc("TRN2", target_bir_lowering=False, num_devices=1)
    arrays = {f"in_{n}": np.ascontiguousarray(inputs[n]) for n in _INS}
    arrays["in_table"] = np.concatenate(list(constants().values()), axis=1)
    args = [nc.dram_tensor(n, a.shape, mybir.dt.from_np(a.dtype), kind="ExternalInput").ap() for n, a in arrays.items()]
    args.append(nc.dram_tensor("out_x", (1, S, D), F32, kind="ExternalOutput").ap())
    build(nc, *args)
    r = _run(nc, [arrays], core_ids=[0])
    return r.results[0]["out_x"]
```
